# Optimizing a Trainium2 kernel written in Bass

```python
import math
import jax, jax.numpy as jnp
from jax import lax
import numpy as np

D_MODEL = 1024
BATCH = 1
SEQ = 256
DEPTH = 2

D_FF = 2816
MLA_HEADS = 4
MLA_Q_LORA = 384
MLA_KV_LORA = 256
MLA_NOPE = 128
MLA_ROPE = 64
MLA_V = 128
MLA_W = MLA_HEADS * MLA_V
MLSTM_HEADS = 4
MLSTM_DH = 128
MLSTM_W = MLSTM_HEADS * MLSTM_DH
MLSTM_CONV = 4
RET_HEADS = 4
RET_DH = 128
RET_W = RET_HEADS * RET_DH
N_BRANCH = 3
Q_BLOCK = 128
CHUNK = 128
ROPE_THETA = 10000.0
NORM_EPS = 1e-5
NEG_INF = -1e30
DN_ALPHA = (2 * DEPTH) ** 0.25
DN_BETA = (8 * DEPTH) ** -0.25
IN_SPLITS = (MLA_Q_LORA, MLA_KV_LORA, MLA_ROPE,
             MLSTM_W, MLSTM_W, MLSTM_W,
             MLSTM_HEADS, MLSTM_HEADS, MLSTM_W,
             RET_W, RET_W, RET_W, RET_W,
             N_BRANCH * D_MODEL)
IN_COLS = sum(IN_SPLITS)

kernel_name = 'hybrid_mla_mlstm_retention_macaron_deepnorm'

def _split_cols(z, sizes):
    out = []
    start = 0
    for n in sizes:
        out.append(z[..., start:start + n])
        start += n
    return out

def _layer_norm(x, g, b):
    xf = x.astype(jnp.float32)
    mu = jnp.mean(xf, axis=-1, keepdims=True)
    var = jnp.mean(jnp.square(xf - mu), axis=-1, keepdims=True)
    return ((xf - mu) * lax.rsqrt(var + NORM_EPS) * g + b).astype(x.dtype)

def _rms_norm(x, g):
    xf = x.astype(jnp.float32)
    y = xf * lax.rsqrt(jnp.mean(jnp.square(xf), axis=-1, keepdims=True) + NORM_EPS)
    return (y * g).astype(x.dtype)

def _head_norm(x, g, n_heads):
    b, s, w = x.shape
    xf = x.astype(jnp.float32).reshape(b, s, n_heads, w // n_heads)
    mu = jnp.mean(xf, axis=-1, keepdims=True)
    var = jnp.mean(jnp.square(xf - mu), axis=-1, keepdims=True)
    y = ((xf - mu) * lax.rsqrt(var + NORM_EPS)).reshape(b, s, w)
    return (y * g).astype(x.dtype)

def _swiglu(x, w_gate, w_up, w_down):
    return (jax.nn.silu(x @ w_gate) * (x @ w_up)) @ w_down

def _rope(x, pos):
    half = x.shape[-1] // 2
    inv_freq = ROPE_THETA ** (-jnp.arange(half, dtype=jnp.float32) / half)
    ang = pos.astype(jnp.float32)[:, :, None, None] * inv_freq
    cos, sin = jnp.cos(ang), jnp.sin(ang)
    xf = x.astype(jnp.float32)
    x1, x2 = xf[..., :half], xf[..., half:]
    return jnp.concatenate([x1 * cos - x2 * sin, x2 * cos + x1 * sin], axis=-1).astype(x.dtype)

def _causal_dwconv(x, w, b):
    k, c = w.shape
    y = lax.conv_general_dilated(x, w[:, None, :], window_strides=(1,), padding=[(k - 1, 0)],
                                 dimension_numbers=('NWC', 'WIO', 'NWC'), feature_group_count=c)
    return y + b

def _to_chunks(t):
    b, s = t.shape[:2]
    t = t.reshape(b, s // CHUNK, CHUNK, *t.shape[2:])
    return jnp.moveaxis(t, 3, 1)

def _from_chunks(t):
    b, h, nc, l, d = t.shape
    return jnp.moveaxis(t, 1, 3).reshape(b, nc * l, h * d)

def _mla_attention(q_nope, q_rope, k_nope, k_rope, v):
    b, s, h, _ = q_nope.shape
    nb = s // Q_BLOCK
    scale = (MLA_NOPE + MLA_ROPE) ** -0.5
    key_pos = jnp.arange(s)

    def blocks(t):
        return jnp.moveaxis(t.reshape(b, nb, Q_BLOCK, *t.shape[2:]), 1, 0)

    def attend(args):
        qn, qr, blk = args
        sc = (jnp.einsum('bqhd,bkhd->bhqk', qn, k_nope)
              + jnp.einsum('bqhd,bkd->bhqk', qr, k_rope)).astype(jnp.float32) * scale
        q_pos = blk * Q_BLOCK + jnp.arange(Q_BLOCK)
        sc = jnp.where(key_pos[None, :] <= q_pos[:, None], sc, NEG_INF)
        p = jax.nn.softmax(sc, axis=-1).astype(v.dtype)
        return jnp.einsum('bhqk,bkhd->bqhd', p, v)

    out = lax.map(attend, (blocks(q_nope), blocks(q_rope), jnp.arange(nb)))
    return jnp.moveaxis(out, 0, 1).reshape(b, s, h * v.shape[-1])

def _mlstm(q, k, v, i_pre, f_pre):
    d = q.shape[-1]
    q, k, v = _to_chunks(q), _to_chunks(k * (d ** -0.5)), _to_chunks(v)
    ig = _to_chunks(i_pre.astype(jnp.float32))
    lf = _to_chunks(jax.nn.log_sigmoid(f_pre.astype(jnp.float32)))
    g = jnp.cumsum(lf, axis=-1)
    g_last = g[..., -1]
    w_loc = g_last[..., None] - g + ig
    m_loc = jnp.max(w_loc, axis=-1)
    e_loc = jnp.exp(w_loc - m_loc[..., None])
    c_loc = jnp.einsum('bhcl,bhcld,bhcle->bhcde', e_loc, k, v)
    n_loc = jnp.einsum('bhcl,bhcld->bhcd', e_loc, k)

    def step(carry, xs):
        c, n, m = carry
        gl, ml, cl, nl = xs
        m_new = jnp.maximum(gl + m, ml)
        a = jnp.exp(gl + m - m_new)
        bsc = jnp.exp(ml - m_new)
        c_new = a[..., None, None] * c + bsc[..., None, None] * cl
        n_new = a[..., None] * n + bsc[..., None] * nl
        return (c_new, n_new, m_new), (c, n, m)

    bb, hh = q.shape[:2]
    init = (jnp.zeros((bb, hh, d, v.shape[-1]), jnp.float32),
            jnp.zeros((bb, hh, d), jnp.float32),
            jnp.zeros((bb, hh), jnp.float32))
    xs = (jnp.moveaxis(g_last, 2, 0), jnp.moveaxis(m_loc, 2, 0),
          jnp.moveaxis(c_loc, 2, 0), jnp.moveaxis(n_loc, 2, 0))
    _, (c_prev, n_prev, m_prev) = lax.scan(step, init, xs)
    c_prev = jnp.moveaxis(c_prev, 0, 2)
    n_prev = jnp.moveaxis(n_prev, 0, 2)
    m_prev = jnp.moveaxis(m_prev, 0, 2)

    causal = jnp.tril(jnp.ones((CHUNK, CHUNK), dtype=bool))
    log_d = jnp.where(causal, g[..., :, None] - g[..., None, :] + ig[..., None, :], -jnp.inf)
    a_inter = g + m_prev[..., None]
    m_j = jnp.maximum(a_inter, jnp.max(log_d, axis=-1))
    p = jnp.exp(log_d - m_j[..., None])
    e_inter = jnp.exp(a_inter - m_j)
    qk = jnp.einsum('bhcjd,bhcsd->bhcjs', q, k) * p
    num = (jnp.einsum('bhcjs,bhcse->bhcje', qk, v)
           + e_inter[..., None] * jnp.einsum('bhcjd,bhcde->bhcje', q, c_prev))
    den = jnp.sum(qk, axis=-1) + e_inter * jnp.einsum('bhcjd,bhcd->bhcj', q, n_prev)
    h = num / jnp.maximum(jnp.abs(den), jnp.exp(-m_j))[..., None]
    return _from_chunks(h)

def _retention(q, k, v):
    d = q.shape[-1]
    n_heads = q.shape[2]
    log_gamma = jnp.log(1.0 - 2.0 ** (-5.0 - jnp.arange(n_heads, dtype=jnp.float32)))
    q, k, v = _to_chunks(q), _to_chunks(k * (d ** -0.5)), _to_chunks(v)
    idx = jnp.arange(CHUNK, dtype=jnp.float32)
    causal = jnp.tril(jnp.ones((CHUNK, CHUNK), dtype=bool))
    decay = jnp.exp(jnp.where(causal, (idx[:, None] - idx[None, :]) * log_gamma[:, None, None], -jnp.inf))
    intra = jnp.einsum('bhcjs,bhcse->bhcje',
                       jnp.einsum('bhcjd,bhcsd->bhcjs', q, k) * decay[None, :, None], v)
    w_state = jnp.exp((CHUNK - 1 - idx)[None, :] * log_gamma[:, None])
    s_loc = jnp.einsum('hl,bhcld,bhcle->bhcde', w_state, k, v)
    g_chunk = jnp.exp(CHUNK * log_gamma)[None, :, None, None]

    def step(r, s_c):
        return g_chunk * r + s_c, r

    r0 = jnp.zeros((q.shape[0], n_heads, d, v.shape[-1]), jnp.float32)
    _, r_prev = lax.scan(step, r0, jnp.moveaxis(s_loc, 2, 0))
    r_prev = jnp.moveaxis(r_prev, 0, 2)
    xi = jnp.exp((idx + 1.0)[None, :] * log_gamma[:, None])
    inter = xi[None, :, None, :, None] * jnp.einsum('bhcjd,bhcde->bhcje', q, r_prev)
    return _from_chunks(intra + inter)

def _hybrid_mixer(x, pos, w_in, mla_q_norm_g, mla_w_uq, mla_kv_norm_g, mla_w_ukv,
                  mlstm_conv_w, mlstm_conv_b, mlstm_gate_b, mlstm_norm_g, ret_norm_g,
                  w_br_mla, w_br_mlstm, w_br_ret, gate_b, w_out):
    b, s, _ = x.shape
    z = x @ w_in
    (c_q, c_kv, k_r, mq, mk, mv, mi, mf, mo, rq, rk, rv, rg, gl) = _split_cols(z, IN_SPLITS)

    qh = (_rms_norm(c_q, mla_q_norm_g) @ mla_w_uq).reshape(b, s, MLA_HEADS, MLA_NOPE + MLA_ROPE)
    q_nope, q_rope = qh[..., :MLA_NOPE], _rope(qh[..., MLA_NOPE:], pos)
    kv = (_rms_norm(c_kv, mla_kv_norm_g) @ mla_w_ukv).reshape(b, s, MLA_HEADS, MLA_NOPE + MLA_V)
    k_nope, v_mla = kv[..., :MLA_NOPE], kv[..., MLA_NOPE:]
    k_rope = _rope(k_r[:, :, None, :], pos)[:, :, 0, :]
    y_mla = _mla_attention(q_nope, q_rope, k_nope, k_rope, v_mla)

    qk_c = jax.nn.silu(_causal_dwconv(jnp.concatenate([mq, mk], axis=-1), mlstm_conv_w, mlstm_conv_b))
    mq_c, mk_c = qk_c[..., :MLSTM_W], qk_c[..., MLSTM_W:]
    gates = jnp.concatenate([mi, mf], axis=-1) + mlstm_gate_b
    i_pre, f_pre = gates[..., :MLSTM_HEADS], gates[..., MLSTM_HEADS:]
    hs = (b, s, MLSTM_HEADS, MLSTM_DH)
    h_ml = _mlstm(mq_c.reshape(hs), mk_c.reshape(hs), mv.reshape(hs), i_pre, f_pre)
    y_mlstm = jax.nn.sigmoid(mo) * _head_norm(h_ml, mlstm_norm_g, MLSTM_HEADS)

    rs = (b, s, RET_HEADS, RET_DH)
    h_rt = _retention(_rope(rq.reshape(rs), pos), _rope(rk.reshape(rs), pos), rv.reshape(rs))
    y_ret = jax.nn.silu(rg) * _head_norm(h_rt, ret_norm_g, RET_HEADS)

    gate = jax.nn.sigmoid(gl.reshape(b, s, N_BRANCH, D_MODEL) + gate_b)
    merged = (gate[:, :, 0] * (y_mla @ w_br_mla)
              + gate[:, :, 1] * (y_mlstm @ w_br_mlstm)
              + gate[:, :, 2] * (y_ret @ w_br_ret))
    return merged @ w_out

def setup_inputs(seed: int = 0) -> dict:
    key = jax.random.key(seed)
    keys = jax.random.split(key, 32)

    def nrm(i, shape, scale):
        return scale * jax.random.normal(keys[i], shape, dtype=jnp.float32)

    def gain(i, n):
        return 1.0 + nrm(i, (DEPTH, n), 0.02)

    offs = jax.random.randint(keys[1], (BATCH, 1), 0, 4096, dtype=jnp.int32)
    positions = (offs + jnp.arange(SEQ, dtype=jnp.int32)[None, :]).astype(jnp.int32)
    f_bias = jnp.linspace(3.0, 6.0, MLSTM_HEADS, dtype=jnp.float32)[None, :] + nrm(15, (DEPTH, MLSTM_HEADS), 0.1)
    mlstm_gate_b = jnp.concatenate([nrm(14, (DEPTH, MLSTM_HEADS), 0.1), f_bias], axis=-1)
    return {
        'x': nrm(0, (BATCH, SEQ, D_MODEL), 1.0),
        'positions': positions,
        'ffn1_w_gate': nrm(2, (DEPTH, D_MODEL, D_FF), D_MODEL ** -0.5),
        'ffn1_w_up': nrm(3, (DEPTH, D_MODEL, D_FF), D_MODEL ** -0.5),
        'ffn1_w_down': nrm(4, (DEPTH, D_FF, D_MODEL), DN_BETA * D_FF ** -0.5),
        'ln1_g': gain(5, D_MODEL),
        'ln1_b': nrm(6, (DEPTH, D_MODEL), 0.02),
        'w_in': nrm(7, (DEPTH, D_MODEL, IN_COLS), D_MODEL ** -0.5),
        'mla_q_norm_g': gain(8, MLA_Q_LORA),
        'mla_w_uq': nrm(9, (DEPTH, MLA_Q_LORA, MLA_HEADS * (MLA_NOPE + MLA_ROPE)), MLA_Q_LORA ** -0.5),
        'mla_kv_norm_g': gain(10, MLA_KV_LORA),
        'mla_w_ukv': nrm(11, (DEPTH, MLA_KV_LORA, MLA_HEADS * (MLA_NOPE + MLA_V)), MLA_KV_LORA ** -0.5),
        'mlstm_conv_w': nrm(12, (DEPTH, MLSTM_CONV, 2 * MLSTM_W), MLSTM_CONV ** -0.5),
        'mlstm_conv_b': nrm(13, (DEPTH, 2 * MLSTM_W), 0.02),
        'mlstm_gate_b': mlstm_gate_b,
        'mlstm_norm_g': gain(16, MLSTM_W),
        'ret_norm_g': gain(17, RET_W),
        'w_br_mla': nrm(18, (DEPTH, MLA_W, D_MODEL), MLA_W ** -0.5),
        'w_br_mlstm': nrm(19, (DEPTH, MLSTM_W, D_MODEL), MLSTM_W ** -0.5),
        'w_br_ret': nrm(20, (DEPTH, RET_W, D_MODEL), RET_W ** -0.5),
        'gate_b': nrm(21, (DEPTH, N_BRANCH, D_MODEL), 0.02),
        'w_out': nrm(22, (DEPTH, D_MODEL, D_MODEL), DN_BETA * D_MODEL ** -0.5),
        'ln2_g': gain(23, D_MODEL),
        'ln2_b': nrm(24, (DEPTH, D_MODEL), 0.02),
        'ffn2_w_gate': nrm(25, (DEPTH, D_MODEL, D_FF), D_MODEL ** -0.5),
        'ffn2_w_up': nrm(26, (DEPTH, D_MODEL, D_FF), D_MODEL ** -0.5),
        'ffn2_w_down': nrm(27, (DEPTH, D_FF, D_MODEL), DN_BETA * D_FF ** -0.5),
        'ln3_g': gain(28, D_MODEL),
        'ln3_b': nrm(29, (DEPTH, D_MODEL), 0.02),
    }

def reference(x, positions, ffn1_w_gate, ffn1_w_up, ffn1_w_down, ln1_g, ln1_b, w_in,
              mla_q_norm_g, mla_w_uq, mla_kv_norm_g, mla_w_ukv, mlstm_conv_w, mlstm_conv_b,
              mlstm_gate_b, mlstm_norm_g, ret_norm_g, w_br_mla, w_br_mlstm, w_br_ret, gate_b,
              w_out, ln2_g, ln2_b, ffn2_w_gate, ffn2_w_up, ffn2_w_down, ln3_g, ln3_b):
    for l in range(DEPTH):
        x = _layer_norm(DN_ALPHA * x + 0.5 * _swiglu(x, ffn1_w_gate[l], ffn1_w_up[l], ffn1_w_down[l]),
                        ln1_g[l], ln1_b[l])
        mix = _hybrid_mixer(x, positions, w_in[l], mla_q_norm_g[l], mla_w_uq[l], mla_kv_norm_g[l],
                            mla_w_ukv[l], mlstm_conv_w[l], mlstm_conv_b[l], mlstm_gate_b[l],
                            mlstm_norm_g[l], ret_norm_g[l], w_br_mla[l], w_br_mlstm[l], w_br_ret[l],
                            gate_b[l], w_out[l])
        x = _layer_norm(DN_ALPHA * x + mix, ln2_g[l], ln2_b[l])
        x = _layer_norm(DN_ALPHA * x + 0.5 * _swiglu(x, ffn2_w_gate[l], ffn2_w_up[l], ffn2_w_down[l]),
                        ln3_g[l], ln3_b[l])
    return x


_drawn_inputs = setup_inputs


def setup_inputs(seed=0):
    import zlib

    import numpy as np

    out = dict(_drawn_inputs(seed))
    spreads = {}
    factors = {'mla_q_norm_g': 8.0,
     'mla_kv_norm_g': 8.0,
     'mlstm_conv_b': 8.0,
     'mlstm_norm_g': 8.0,
     'ret_norm_g': 8.0,
     'gate_b': 8.0}
    for name, (base, spread) in spreads.items():
        noise = np.random.default_rng([zlib.crc32(name.encode()), seed]).standard_normal(out[name].shape)
        drawn = base * np.exp(spread * noise) if base else spread * noise
        out[name] = __import__('jax').numpy.asarray(drawn.astype(out[name].dtype))
    for name, factor in factors.items():
        out[name] = (out[name] * factor).astype(out[name].dtype)
    return out
```

```python
from contextlib import ExitStack

import concourse.bass as bass
import numpy as np
from concourse import mybir

F32 = mybir.dt.float32
F32R = mybir.dt.float32r
I32 = mybir.dt.int32
ALU = mybir.AluOpType
ACT = mybir.ActivationFunctionType
AX = mybir.AxisListType

P = 128
DEPTH, SEQ, D_MODEL, D_FF = 2, 256, 1024, 2816
TT = SEQ // P
KC = D_MODEL // P
HEADS, DH = 4, 128
ROPE = 64
Q_LORA, KV_LORA = 384, 256
QC, VC = Q_LORA // P, KV_LORA // P
CONV = 4
EPS = 1e-5
ALPHA = (2 * DEPTH) ** 0.25
MLA_SCALE = (DH + ROPE) ** -0.5
HEAD_SCALE = DH ** -0.5
NEG = -1e30
THETA = 10000.0

FB = 256
NF = D_FF // FB
UNIT = 2048
RING = 3
U_FFN = 3 * NF
MIX_FIXED, MIX_LOOP, MIX_OUT = 23, 18, 4
U_MIX = MIX_FIXED + MIX_LOOP + MIX_OUT
U_LAYER = 2 * U_FFN + U_MIX
FFN_BASE = (0, U_FFN + U_MIX)
MIX_BASE = U_FFN
assert U_LAYER % RING == 0 and U_FFN % RING == 0 and U_MIX % RING == 0

C_MQ, C_MV, C_GATES, C_MO = 704, 1728, 2240, 2248
C_RQ, C_RK, C_RV, C_RG, C_GL = 2760, 3272, 3784, 4296, 4808

PARAM_SIZES = dict(ln_g=24, ln_b=24, q_g=QC, kv_g=VC, conv_w=CONV * 8, conv_b=8, ml_g=4, rt_g=4,
                   gate_b=24, i_b=1, f_b=1)
PARAM_AT, NPAR = {}, 0
for _name, _n in PARAM_SIZES.items():
    PARAM_AT[_name] = NPAR
    NPAR += _n

CONST_SIZES = dict(ident=P, ones=P, mask=384, pmask=384, decay=HEADS * 384, sel=HEADS * P,
                   invf=2, sign=2, eps=2, one=1)
CONST_AT, NCONST = {}, 0
for _name, _n in CONST_SIZES.items():
    CONST_AT[_name] = NCONST
    NCONST += _n

TWO_PI = 2 * np.pi
PI_A = float(np.float32(6.28125))
PI_B = float(np.float32(np.round((TWO_PI - PI_A) * 2 ** 19) / 2 ** 19))
PI_C = float(np.float32(TWO_PI - PI_A - PI_B))
PI_MAX = 3.1415925
ANGLE_STEPS = 9
ROUND = 1.5 * 2.0 ** 23


def constants():
    c = np.zeros((P, NCONST), np.float32)
    at = CONST_AT
    i = np.arange(P)
    c[:, at["ident"]:at["ident"] + P] = np.eye(P)
    c[:, at["ones"]:at["ones"] + P] = 1.0
    lower = np.where(i[None, :] <= i[:, None], 0.0, NEG)
    c[:, at["mask"]:at["mask"] + 128] = lower
    c[:, at["mask"] + 256:at["mask"] + 384] = lower
    upper = np.where(i[None, :] >= i[:, None], 0.0, -NEG)
    c[:, at["pmask"]:at["pmask"] + 128] = upper
    c[:, at["pmask"] + 256:at["pmask"] + 384] = upper
    for h in range(HEADS):
        lg = np.log(1.0 - 2.0 ** (-5.0 - h))
        d = (i[None, :] - i[:, None]).astype(np.float64)
        o = at["decay"] + 384 * h
        c[:, o:o + 128] = c[:, o + 256:o + 384] = np.where(d >= 0, np.exp(lg * d), 0.0)
        c[:, o + 128:o + 256] = np.exp(lg * (d + 128))
        c[h, at["sel"] + h * P:at["sel"] + (h + 1) * P] = 1.0
    for n, half in enumerate((DH // 2, ROPE // 2)):
        c[:, at["invf"] + n] = np.float32(THETA) ** (-(i % half).astype(np.float32) / np.float32(half))
        c[:, at["sign"] + n] = np.where(i % (2 * half) < half, -1.0, 1.0)
    c[:, at["eps"]] = EPS
    c[:, at["eps"] + 1] = EPS / 0.25
    c[:, at["one"]] = 1.0
    return c


def build(nc, a):
    ctx = ExitStack()
    at = [nc.sbuf_base + 31 & ~31]

    def place(name, shape, dt, offset):
        return nc.alloc_sbuf_tensor_at(name, shape, dt, offset=offset)

    def sb(name, shape, dt=F32):
        t = place(name, shape, dt, at[0])
        at[0] += 4 * int(np.prod(shape[1:])) + 31 & ~31
        return t

    def region(nbytes):
        start = at[0]
        at[0] += nbytes
        return start

    def sem(name):
        return ctx.enter_context(nc.semaphore(name))

    cst = sb("cst", [P, NCONST])
    par_all = sb("par_all", [P, DEPTH, NPAR])
    par = sb("par", [P, NPAR])
    cos_r, sin_r = sb("cos_r", [P, SEQ]), sb("sin_r", [P, SEQ])
    cos_m, sin_m = sb("cos_m", [P, SEQ]), sb("sin_m", [P, SEQ])
    raw = sb("raw", [P, RING, UNIT])
    whi, wlo = sb("whi", [P, RING, UNIT], F32R), sb("wlo", [P, RING, UNIT], F32R)
    xhi, xlo = sb("xhi", [P, KC, SEQ], F32R), sb("xlo", [P, KC, SEQ], F32R)
    xtok = sb("xtok", [P, TT, D_MODEL])
    stats = sb("stats", [P, TT, 2, 6])
    mv = sb("mv", [P, TT, 2])
    std = sb("std", [P, TT])
    rstd = sb("rstd", [P, TT])
    mx = sb("mx", [P, HEADS, 2])
    rowsum = sb("rowsum", [P, HEADS, 2])
    rinv = sb("rinv", [P, HEADS, 2])
    a_col = sb("a_col", [P, TT, HEADS])
    gb_col = sb("gb_col", [P, KC])
    pause = sb("pause", [P, 1])

    r_u2, r_rows, r_y, r_b = region(24576), region(5120), region(24576), region(15360)
    r_qk, r_mv, r_rq, r_rk = region(8192), region(4096), region(4096), region(4096)
    assert at[0] <= nc.sbuf_top, (at[0], nc.sbuf_top)
    silu = place("silu", [P, 2 * SEQ], F32, r_u2)
    hid = place("hid", [P, 2 * SEQ], F32, r_u2 + 2048)
    hhi = place("hhi", [P, 2 * SEQ], F32R, r_u2 + 4096)
    hlo = place("hlo", [P, 2 * SEQ], F32R, r_u2 + 6144)
    z = place("z", [P, TT, D_MODEL], F32, r_u2)
    xf = place("xf", [P, KC, SEQ], F32, r_u2 + 8192)
    g_row = place("g_row", [P, D_MODEL], F32, r_u2 + 16384)
    b_row = place("b_row", [P, D_MODEL], F32, r_u2 + 20480)
    PADW = SEQ + CONV - 1
    conv_in = place("conv_in", [P, 8, PADW], F32, r_u2)
    rv = place("rv", [P, TT, HEADS * DH], F32, r_u2)
    rg = place("rg", [P, HEADS, SEQ], F32, r_u2 + 4096)
    rot = place("rot", [P, 2 * SEQ], F32, r_u2 + 8320)
    rot_sw = place("rot_sw", [P, 2 * SEQ], F32, r_u2 + 10368)
    bc = place("bc", [P, 2, 2 * SEQ], F32, r_u2 + 12416)
    sc = place("sc", [P, 2, 384], F32, r_u2 + 16512)
    pt = place("pt", [P, 2, 384], F32, r_u2 + 19584)
    row_i = place("row_i", [HEADS, SEQ], F32, r_rows)
    row_f = place("row_f", [HEADS, SEQ], F32, r_rows + 1024)
    row_t = place("row_t", [HEADS, SEQ], F32, r_rows + 2048)
    row_m = place("row_m", [HEADS, 2 * SEQ], F32, r_rows + 3072)
    lat = place("lat", [P, QC + VC, SEQ], F32, r_y)
    lat_sq = place("lat_sq", [P, QC + VC, SEQ], F32, r_y + 5120)
    lhi = place("lhi", [P, QC + VC, SEQ], F32R, r_y + 10240)
    llo = place("llo", [P, QC + VC, SEQ], F32R, r_y + 15360)
    yhi = place("yhi", [P, 3, HEADS, SEQ], F32R, r_y)
    ylo = place("ylo", [P, 3, HEADS, SEQ], F32R, r_y + 12288)
    mhi = place("mhi", [P, KC, SEQ], F32R, r_y)
    mlo = place("mlo", [P, KC, SEQ], F32R, r_y + 8192)
    k_rope = place("k_rope", [P, SEQ], F32, r_b)
    q_nope = place("q_nope", [P, HEADS, SEQ], F32, r_b + 1024)
    q_rope = place("q_rope", [P, 2, SEQ], F32, r_b + 5120)
    k_nope = place("k_nope", [P, HEADS, SEQ], F32, r_b + 7168)
    v_mla = place("v_mla", [P, TT, HEADS * DH], F32, r_b + 11264)
    ht = place("ht", [P, 2, 2 * SEQ], F32, r_b)
    ht_sq = place("ht_sq", [P, 2 * SEQ], F32, r_b + 4096)
    ht_rs = place("ht_rs", [P, 2 * SEQ], F32, r_b + 6144)
    mo = place("mo", [P, HEADS, SEQ], F32, r_b + 8192)
    lat_rs = place("lat_rs", [P, 2 * SEQ], F32, r_b + 13312)
    ml_qk = place("ml_qk", [P, 8, SEQ], F32, r_qk)
    merged = place("merged", [P, KC, SEQ], F32, r_qk)
    ml_v = place("ml_v", [P, TT, HEADS * DH], F32, r_mv)
    gate = place("gate", [P, 4, SEQ], F32, r_mv)
    rq = place("rq", [P, HEADS, SEQ], F32, r_rq)
    rk = place("rk", [P, HEADS, SEQ], F32, r_rk)
    pos_i = place("pos_i", [P, SEQ], I32, r_y)
    pos_f = place("pos_f", [P, SEQ], F32, r_y + 1024)
    ang = place("ang", [P, SEQ], F32, r_y + 2048)
    turns = place("turns", [P, SEQ], F32, r_y + 3072)

    ps = ctx.enter_context(nc.psum_tensor("ps", [P, 8, 512], F32))

    def C(name, n=None, off=0):
        o = CONST_AT[name] + off
        return cst[:, o:o + (n or CONST_SIZES[name])]

    def par_col(name, n):
        o = PARAM_AT[name] + n
        return par[:, o:o + 1]

    ident, ones = C("ident"), C("ones")

    const_loaded, x_loaded, out_stored = sem("const_loaded"), sem("x_loaded"), sem("out_stored")
    w_loaded = [sem(f"w_loaded{s}") for s in range(RING)]
    w_hi, w_lo, w_used = sem("w_hi"), sem("w_lo"), sem("w_used")
    angle_step, sin_ready, sign_ready = sem("angle_step"), sem("sin_ready"), sem("sign_ready")
    x_turned, x_copied = sem("x_turned"), sem("x_copied")
    par_ready = sem("par_ready")
    silu_done, prod_done, hid_hi, hid_lo = sem("silu_done"), sem("prod_done"), sem("hid_hi"), sem("hid_lo")
    y_cleared = sem("y_cleared")
    rows_loaded = sem("rows_loaded")
    ln_sum, ln_stats, ln_var, ln_std = sem("ln_sum"), sem("ln_stats"), sem("ln_var"), sem("ln_std")
    ln_rstd, ln_rows, ln_turned = sem("ln_rstd"), sem("ln_rows"), sem("ln_turned")
    x_act, x_dve, rows_scaled, xtok_ready = sem("x_act"), sem("x_dve"), sem("rows_scaled"), sem("xtok_ready")
    x_hi, x_ready = sem("x_hi"), sem("x_ready")
    lat_copied, lat_squared, lat_summed = sem("lat_copied"), sem("lat_squared"), sem("lat_summed")
    lat_std, lat_rstd, lat_scaled = sem("lat_std"), sem("lat_rstd"), sem("lat_scaled")
    lat_hi, lat_lo = sem("lat_hi"), sem("lat_lo")
    rot_copied, rot_parts, rotated = sem("rot_copied"), sem("rot_parts"), sem("rotated")
    conv_pad, conv_copied, conv_tap, qk_silu = sem("conv_pad"), sem("conv_copied"), sem("conv_tap"), sem("qk_silu")
    q_copied, k_copied, v_copied = sem("q_copied"), sem("k_copied"), sem("v_copied")
    mo_ready, rg_ready = sem("mo_ready"), sem("rg_ready")
    s_done, s_masked, s_max, s_negmax = sem("s_done"), sem("s_masked"), sem("s_max"), sem("s_negmax")
    s_exp, s_rsum, s_probs = sem("s_exp"), sem("s_rsum"), sem("s_probs")
    p_turned, p_copied, mla_done = sem("p_turned"), sem("p_copied"), sem("mla_done")
    f_pre, f_abs, f_exp, f_log = sem("f_pre"), sem("f_abs"), sem("f_exp"), sem("f_log")
    log_f, g_row_ready, a_row_ready, m_row_ready = sem("log_f"), sem("g_row"), sem("a_row"), sem("m_row")
    gm_row_ready, floor_ready, a_turned, a_copied = sem("gm_row"), sem("floor_row"), sem("a_turned"), sem("a_copied")
    bc_done, bc_copied, decay_arg, decay_ready = sem("bc_done"), sem("bc_copied"), sem("decay_arg"), sem("decay_ready")
    ml_scored, ml_probs, ml_summed = sem("ml_scored"), sem("ml_probs"), sem("ml_summed")
    den_step, h_ready = sem("den_step"), sem("h_ready")
    rt_scored, rt_probs, rt_summed, rt_copied = sem("rt_scored"), sem("rt_probs"), sem("rt_summed"), sem("rt_copied")
    h_means, h_centred, h_squared, h_vars = sem("h_means"), sem("h_centred"), sem("h_squared"), sem("h_vars")
    h_std, h_rstd, h_scaled, h_gated = sem("h_std"), sem("h_rstd"), sem("h_scaled"), sem("h_gated")
    y_hi, y_lo = sem("y_hi"), sem("y_lo")
    bias_copied, gates_ready, gate_used = sem("bias_copied"), sem("gates_ready"), sem("gate_used")
    branch_added, merge_zero, m_hi, m_lo = sem("branch_added"), sem("merge_zero"), sem("m_hi"), sem("m_lo")

    def unit_no(l, k, f=0):
        return l * U_LAYER + f * RING + (k + 1)

    def loaded_no(l, k, f=0):
        return (l * (U_LAYER // RING) + f + (k // RING + 1)) * 16

    free_no = unit_no

    def done_no(l, k, f=0):
        return unit_no(l, k, f) + RING

    def step_no(l, w, f):
        return l * (2 * NF) + f + (w * NF + 1)

    MIX_SIZE = ([2048, 2048, KC * 192] + [2048] * 4 + [QC * 384] * 2 + [VC * 1024] + [2048] * 2
                + [KC * 2 * HEADS] + [2048] * (MIX_FIXED - 13 + MIX_LOOP + MIX_OUT))

    def size_of(k):
        return MIX_SIZE[k - MIX_BASE] if MIX_BASE <= k < MIX_BASE + U_MIX else UNIT

    def flat(ap):
        return ap.rearrange("p a b -> p (a b)")

    def halves(ap):
        return ap.rearrange("p (a b) -> p a b", a=2)

    def twice(table):
        return table[:, :].unsqueeze(1).broadcast_to([P, 2, SEQ])

    PROJ = ["c0", "c1", "c2", "qk0", "qk1", "qk2", "qk3", "qn0", "qr", "qn1", "kn0", "kn1", "v0", "v1",
            "mv0", "mv1", "gates", "rq0", "rq1", "rk0", "rk1", "rv0", "rv1", "mo0", "mo1", "rg0", "rg1"]
    SMALL = ["rms", "S0", "S1", "T0", "T1", "pv0", "S2", "S3", "aT", "T2", "T3", "bc0", "bc1", "pv1",
             "mS0", "mS1", "mpv0", "mpv1", "bc2", "bc3", "m_mean0", "mS2", "mS3", "m_var0", "mpv2", "mpv3",
             "rS0", "rS1", "m_mean1", "rpv0", "rS2", "rS3", "m_var1", "r_mean0", "rpv1", "r_var0",
             "r_mean1", "r_var1"]
    BANK = {n: 4 + i % 4 for i, n in enumerate(PROJ)} | {n: i % 4 for i, n in enumerate(SMALL)}

    block = ctx.enter_context(nc.Block())

    @block.sync
    def _(sp):
        for s, n in ((w_used, RING), (w_lo, RING), (prod_done, 1), (hid_lo, 1),
                     (xtok_ready, 1), (gates_ready, 1), (branch_added, 1)):
            sp.sem_inc(s, n)
        sp.dma_start(xtok[:, :, :], a["x"].rearrange("b (t p) d -> p (b t) d", p=P)).then_inc(x_loaded, 16)
        sp.dma_start(cst[:, :], a["consts"][:, :]).then_inc(const_loaded, 16)
        sp.dma_start(pos_i[:, :], a["positions"][0, :].partition_broadcast(P)).then_inc(const_loaded, 16)
        sp.dma_start(par_all[:, :, :], a["params"].rearrange("l p n -> p l n")).then_inc(const_loaded, 16)

        def load(l, k, src, shape, f=0):
            n = int(np.prod(shape))
            sp.wait_ge(w_lo, free_no(l, k, f))
            sp.dma_start(raw[:, k % RING, 0:n].rearrange("p (a b) -> p a b", a=shape[0]), src)\
              .then_inc(w_loaded[k % RING], 16)

        def chunks(src):
            return src.rearrange("(k p) n -> p k n", p=P)

        def load_in(l, m, lo, n):
            load(l, MIX_BASE + m, chunks(a["w_in"][l, :, lo:lo + n]), (KC, n))

        def load_rows(l, w):
            sp.wait_ge(xtok_ready, l * 6 + (2 * w + 1))
            if w == 1:
                sp.wait_ge(rt_summed, l * 2 + 2)
            for i, dst in enumerate((g_row, b_row)):
                sp.dma_start(dst[:, :], a["ln_rows"][l, w, i, :].partition_broadcast(P)).then_inc(rows_loaded, 16)

        def ffn(l, w):
            base = FFN_BASE[w]
            wg, wu, wd = (a[f"ffn{w + 1}_w_{n}"] for n in ("gate", "up", "down"))

            def cols(src, f):
                return chunks(src[l, :, bass.ds(f * FB, FB)])

            def rows(f):
                return chunks(wd[l, bass.ds(f * FB, FB), :])

            load(l, base, cols(wg, 0), (KC, FB))
            load(l, base + 1, cols(wu, 0), (KC, FB))
            with sp.Fori(0, NF - 1) as f:
                load(l, base + 2, cols(wg, f + 1), (KC, FB), f)
                load(l, base + 3, cols(wu, f + 1), (KC, FB), f)
                load(l, base + 4, rows(f), (2, D_MODEL), f)
            load_rows(l, 2 * w)
            load(l, base + 3 * NF - 1, rows(NF - 1), (2, D_MODEL))

        def mixer(l):
            load_in(l, 0, 0, 256)
            load_in(l, 1, 256, 256)
            load_in(l, 2, 512, 192)
            for i in range(4):
                load_in(l, 3 + i, C_MQ + 256 * i, 256)
            for i in range(2):
                load(l, MIX_BASE + 7 + i, chunks(a["mla_w_uq"][l, :, 384 * i:384 * i + 384]), (QC, 384))
            load(l, MIX_BASE + 9, chunks(a["mla_w_ukv"][l, :, :]), (VC, 1024))
            for i in range(2):
                load_in(l, 10 + i, C_MV + 256 * i, 256)
            load_in(l, 12, C_GATES, 2 * HEADS)
            for m, c in ((13, C_RQ), (15, C_RK), (17, C_RV), (19, C_MO), (21, C_RG)):
                for i in range(2):
                    load_in(l, m + i, c + 256 * i, 256)
            with sp.Fori(0, 3) as b:
                for h in range(2):
                    for i in range(2):
                        start = C_GL + 512 * h + 256 * i
                        load(l, MIX_BASE + 23 + 3 * h + i,
                             chunks(a["w_in"][l, :, bass.ds(b * D_MODEL + start, 256)]), (KC, 256), b * 2)
                    load(l, MIX_BASE + 25 + 3 * h, chunks(a["w_br"][l, b, :, 512 * h:512 * h + 512]),
                         (HEADS, 512), b * 2)
            load_rows(l, 1)
            for i in range(MIX_OUT):
                load(l, MIX_BASE + 41 + i, chunks(a["w_out"][l, 256 * i:256 * i + 256, :]), (2, D_MODEL))

        with sp.Fori(0, DEPTH) as l:
            ffn(l, 0)
            mixer(l)
            ffn(l, 1)
        sp.wait_ge(xtok_ready, DEPTH * 6 + 1)
        sp.dma_start(a["out"].rearrange("b (t p) d -> p (b t) d", p=P), xtok[:, :, :]).then_inc(out_stored, 16)
        sp.wait_ge(out_stored, 16)

    @block.gpsimd
    def _(pool):
        with pool.Fori(0, DEPTH) as l:
            for w in range(3):
                pool.wait_ge(rows_loaded, l * 96 + 32 * (w + 1))
                for t in range(TT):
                    pool.wait_ge(ln_rows, l * 6 + (2 * w + t + 1))
                    pool.tensor_tensor(xtok[:, t, :], z[:, t, :], g_row[:, :], ALU.mult).then_inc(rows_scaled, 1)
                for t in range(TT):
                    pool.wait_ge(rows_scaled, l * 6 + (2 * w + t + 1))
                    pool.tensor_tensor(xtok[:, t, :], xtok[:, t, :], b_row[:, :], ALU.add).then_inc(xtok_ready, 1)

    @block.scalar
    def _(act):
        def hi(l, k, f=0):
            n = size_of(k)
            act.wait_ge(w_loaded[k % RING], loaded_no(l, k, f))
            act.wait_ge(w_used, free_no(l, k, f))
            act.activation(whi[:, k % RING, 0:n], raw[:, k % RING, 0:n], ACT.Copy).then_inc(w_hi, 1)

        def ffn(l, w):
            base = FFN_BASE[w]
            if w == 0:
                hi(l, base)
                hi(l, base + 1)
            act.wait_ge(xtok_ready, l * 6 + (4 * w + 1))

            def silu_of(j, k, f):
                act.wait_ge(w_used, done_no(l, k, f))
                act.wait_ge(prod_done, step_no(l, w, j))
                act.activation(silu[:, :], ps[:, 4, :], ACT.Silu).then_inc(silu_done, 1)

            hi(l, base + 2)
            silu_of(0, base, 0)
            hi(l, base + 3)
            hi(l, base + 4)
            with act.Fori(0, NF - 2) as f:
                hi(l, base + 5, f)
                silu_of(f + 1, base + 2, f)
                hi(l, base + 6, f)
                hi(l, base + 7, f)
            silu_of(NF - 1, base + 2, NF - 2)
            hi(l, base + 3 * NF - 1)

        def layer_norm(l, w, early):
            for k in early[:2]:
                hi(l, k)
            for t in range(TT):
                act.wait_ge(ln_var, l * 6 + (2 * w + t + 1))
                act.activation(std[:, t:t + 1], mv[:, t, 1:2], ACT.Sqrt,
                               bias=C("eps", 1, 0 if w == 1 else 1)).then_inc(ln_std, 1)
            for k in early[2:]:
                hi(l, k)
            act.wait_ge(ln_turned, l * 6 + (2 * w + 2))
            for k in range(4):
                act.activation(xf[:, k, :], ps[:, 4 + k // 2, (k % 2) * SEQ:(k % 2 + 1) * SEQ], ACT.Identity,
                               bias=par_col("ln_b", 8 * w + k), scale=par_col("ln_g", 8 * w + k)).then_inc(x_act, 1)

        def mixer(l):
            m0 = MIX_BASE

            def copy(dst, job, lo=0, n=512, func=ACT.Copy, src=slice(0, P)):
                return act.activation(dst, ps[src, BANK[job], lo:lo + n], func)

            def swap(job, half):
                copy(rot[:, :], job)
                for p0 in range(0, P, half):
                    p1 = p0 ^ half
                    last = copy(rot_sw[p0:p0 + half, :], job, src=slice(p1, p1 + half))
                return last

            def exps(h):
                act.wait_ge(s_negmax, l * 4 + (h + 1))
                for q, (c0, c1) in enumerate(((0, P), (P, 3 * P))):
                    last = act.activation(sc[:, h % 2, c0:c1], sc[:, h % 2, c0:c1], ACT.Exp,
                                          bias=mx[:, h, q:q + 1], accum_out=rowsum[:, h, q:q + 1])
                last.then_inc(s_exp, 1)

            def pt_copy(h):
                act.wait_ge(p_turned, l * 4 + (h + 1))
                copy(pt[:, h % 2, :], f"T{h}", 0, 384).then_inc(p_copied, 1)

            def bc_copy(h):
                act.wait_ge(bc_done, l * 4 + (h + 1))
                copy(bc[:, h % 2, :], f"bc{h}").then_inc(bc_copied, 1)

            def decay(h):
                act.wait_ge(decay_arg, l * 4 + (h + 1))
                act.activation(sc[:, h % 2, :], sc[:, h % 2, :], ACT.Exp, scale=-1.0).then_inc(decay_ready, 1)

            def norm_std(n):
                act.wait_ge(h_vars, l * 4 + (n + 1))
                if n:
                    act.wait_ge(h_scaled, l * 4 + n)
                act.activation(ht_rs[:, :], ps[:, BANK[f"{'mr'[n // 2]}_var{n % 2}"], :], ACT.Sqrt,
                               scale=1.0 / DH, bias=C("eps", 1)).then_inc(h_std, 1)

            hi(l, m0 + 3)
            act.wait_ge(w_used, done_no(l, m0))
            copy(flat(lat[:, 0:2, :]), "c0").then_inc(lat_copied, 1)
            hi(l, m0 + 4)
            act.wait_ge(w_used, done_no(l, m0 + 1))
            copy(flat(lat[:, 2:4, :]), "c1").then_inc(lat_copied, 1)
            hi(l, m0 + 5)
            act.wait_ge(w_used, done_no(l, m0 + 2))
            copy(lat[:, 4, :], "c2", 0, SEQ).then_inc(lat_copied, 1)
            for p0 in (0, ROPE):
                copy(rot[p0:p0 + ROPE, 0:SEQ], "c2", SEQ, SEQ, src=slice(0, ROPE))
            for i in range(4):
                p0, p1 = 32 * i, 32 * (1 - i % 2)
                last = copy(rot_sw[p0:p0 + 32, 0:SEQ], "c2", SEQ, SEQ, src=slice(p1, p1 + 32))
            last.then_inc(rot_copied, 1)
            hi(l, m0 + 6)
            act.wait_ge(lat_summed, l + 1)
            act.activation(lat_rs[:, 0:SEQ], ps[:, BANK["rms"], 0:SEQ], ACT.Sqrt, scale=1.0 / Q_LORA, bias=C("eps", 1))
            act.activation(lat_rs[:, SEQ:], ps[:, BANK["rms"], SEQ:], ACT.Sqrt, scale=1.0 / KV_LORA,
                           bias=C("eps", 1)).then_inc(lat_std, 1)
            act.wait_ge(xtok_ready, l * 6 + 3)
            for i in range(4):
                act.wait_ge(w_used, done_no(l, m0 + 3 + i))
                act.activation(conv_in[:, 2 * i:2 * i + 2, CONV - 1:PADW], halves(ps[:, BANK[f"qk{i}"], :]),
                               ACT.Copy).then_inc(conv_copied, 1)
                hi(l, m0 + 7 + i)
            act.wait_ge(w_used, done_no(l, m0 + 7))
            copy(flat(q_nope[:, 0:2, :]), "qn0").then_inc(q_copied, 1)
            act.wait_ge(conv_tap, l * 32 + 16)
            act.activation(ml_qk[:, 0:4, :], ml_qk[:, 0:4, :], ACT.Silu).then_inc(qk_silu, 1)
            hi(l, m0 + 11)
            act.wait_ge(w_used, done_no(l, m0 + 8))
            act.wait_ge(rotated, l * 6 + 1)
            swap("qr", 32).then_inc(rot_copied, 1)
            copy(flat(q_nope[:, 2:4, :]), "qn1").then_inc(q_copied, 1)
            hi(l, m0 + 12)
            act.wait_ge(w_used, done_no(l, m0 + 9))
            copy(flat(k_nope[:, 0:2, :]), "kn0").then_inc(k_copied, 1)
            copy(flat(k_nope[:, 2:4, :]), "kn1").then_inc(k_copied, 1)
            hi(l, m0 + 13)
            act.wait_ge(conv_tap, l * 32 + 32)
            act.activation(ml_qk[:, 4:8, :], ml_qk[:, 4:8, :], ACT.Silu).then_inc(qk_silu, 1)
            hi(l, m0 + 14)
            exps(0)
            exps(1)
            hi(l, m0 + 15)
            act.wait_ge(f_abs, l + 1)
            act.activation(row_t[:, :], row_t[:, :], ACT.Exp, scale=-1.0).then_inc(f_exp, 1)
            act.wait_ge(f_exp, l + 1)
            act.activation(row_t[:, :], row_t[:, :], ACT.Ln, bias=C("one")[0:HEADS, :]).then_inc(f_log, 1)
            pt_copy(0)
            pt_copy(1)
            hi(l, m0 + 16)
            act.wait_ge(gm_row_ready, l + 1)
            act.activation(row_m[:, SEQ:], row_t[:, :], ACT.Exp, scale=-1.0).then_inc(floor_ready, 1)
            act.wait_ge(w_used, done_no(l, m0 + 13))
            act.wait_ge(rotated, l * 6 + 2)
            swap("rq0", 64).then_inc(rot_copied, 1)
            exps(2)
            exps(3)
            hi(l, m0 + 17)
            act.wait_ge(w_used, done_no(l, m0 + 14))
            act.wait_ge(rotated, l * 6 + 3)
            swap("rq1", 64).then_inc(rot_copied, 1)
            act.wait_ge(mla_done, l * 2 + 1)
            pt_copy(2)
            pt_copy(3)
            hi(l, m0 + 18)
            bc_copy(0)
            bc_copy(1)
            act.wait_ge(w_used, done_no(l, m0 + 15))
            act.wait_ge(rotated, l * 6 + 4)
            swap("rk0", 64).then_inc(rot_copied, 1)
            decay(0)
            decay(1)
            hi(l, m0 + 19)
            act.wait_ge(w_used, done_no(l, m0 + 16))
            act.wait_ge(rotated, l * 6 + 5)
            swap("rk1", 64).then_inc(rot_copied, 1)
            hi(l, m0 + 20)
            act.wait_ge(h_ready, l * 4 + 2)
            bc_copy(2)
            bc_copy(3)
            hi(l, m0 + 21)
            decay(2)
            decay(3)
            norm_std(0)
            hi(l, m0 + 22)
            act.wait_ge(w_used, done_no(l, m0 + 19))
            copy(flat(mo[:, 0:2, :]), "mo0", func=ACT.Sigmoid).then_inc(mo_ready, 1)
            hi(l, m0 + 23)
            act.wait_ge(w_used, done_no(l, m0 + 20))
            copy(flat(mo[:, 2:4, :]), "mo1", func=ACT.Sigmoid).then_inc(mo_ready, 1)
            norm_std(1)
            hi(l, m0 + 24)
            act.wait_ge(w_used, done_no(l, m0 + 21))
            copy(flat(rg[:, 0:2, :]), "rg0", func=ACT.Silu).then_inc(rg_ready, 1)
            norm_std(2)
            hi(l, m0 + 25)
            act.wait_ge(w_used, done_no(l, m0 + 22))
            copy(flat(rg[:, 2:4, :]), "rg1", func=ACT.Silu).then_inc(rg_ready, 1)
            norm_std(3)

            with act.Fori(0, 3) as b:
                turn = l * 3 + b
                act.wait_ge(gates_ready, turn * 4 + 1)
                act.activation(gb_col[:, :], par[:, bass.ds(b * KC + PARAM_AT["gate_b"], KC)],
                               ACT.Copy).then_inc(bias_copied, 1)
                act.wait_ge(bias_copied, turn + 1)
                for h in range(2):
                    for i in range(3):
                        hi(l, m0 + 26 + 3 * h + i, b * 2)
                        if i == 2:
                            continue
                        act.wait_ge(w_used, done_no(l, m0 + 23 + 3 * h + i, b * 2))
                        act.wait_ge(branch_added, turn * 4 + (2 + i if h else 1))
                        if not h:
                            act.wait_ge(ml_summed, l * 4 + 4)
                        for c in range(2):
                            n = 4 * h + 2 * i + c
                            last = act.activation(gate[:, 2 * i + c, :], ps[:, 4 + i, c * SEQ:(c + 1) * SEQ],
                                                  ACT.Sigmoid, bias=gb_col[:, n:n + 1])
                        last.then_inc(gates_ready, 1)
            hi(l, m0 + 44)

        act.wait_ge(x_turned, 1)
        for j in range(4):
            act.activation(flat(xf[:, 2 * j:2 * j + 2, :]), ps[:, 4 + j, :], ACT.Copy).then_inc(x_copied, 1)
        for n, table in enumerate((cos_r, sin_r, cos_m, sin_m)):
            act.wait_ge(angle_step, ANGLE_STEPS * (n + 1) + 1)
            act.activation(table[:, :], table[:, :], ACT.Sin).then_inc(sin_ready, 1)

        with act.Fori(0, DEPTH) as l:
            ffn(l, 0)
            layer_norm(l, 0, [MIX_BASE, MIX_BASE + 1, MIX_BASE + 2])
            mixer(l)
            layer_norm(l, 1, [FFN_BASE[1], FFN_BASE[1] + 1])
            ffn(l, 1)
            layer_norm(l, 2, [])

    @block.vector
    def _(dve):
        def lo(l, k, f=0):
            n = size_of(k)
            dve.wait_ge(w_hi, unit_no(l, k, f))
            dve.tensor_tensor(wlo[:, k % RING, 0:n], raw[:, k % RING, 0:n],
                              whi[:, k % RING, 0:n].bitcast(F32), ALU.subtract).then_inc(w_lo, 1)

        def ffn(l, w):
            base = FFN_BASE[w]
            dve.memset(ps[:, 0:4, :], 0.0).then_inc(y_cleared, 1)
            if w == 0:
                lo(l, base)
                lo(l, base + 1)
            dve.wait_ge(xtok_ready, l * 6 + (4 * w + 1))

            def product(j, k, f):
                dve.wait_ge(silu_done, step_no(l, w, j))
                dve.wait_ge(w_used, done_no(l, k, f))
                dve.wait_ge(hid_lo, step_no(l, w, j))
                dve.tensor_tensor(hid[:, :], silu[:, :], ps[:, 5, :], ALU.mult).then_inc(prod_done, 1)

            def split(j, f):
                dve.wait_ge(prod_done, step_no(l, w, j) + 1)
                if f is not None:
                    dve.wait_ge(w_used, done_no(l, base + 4, f))
                dve.tensor_copy(hhi[:, :], hid[:, :]).then_inc(hid_hi, 1)
                dve.wait_ge(hid_hi, step_no(l, w, j))
                dve.tensor_tensor(hlo[:, :], hid[:, :], hhi[:, :].bitcast(F32), ALU.subtract).then_inc(hid_lo, 1)

            lo(l, base + 2)
            product(0, base + 1, 0)
            lo(l, base + 3)
            split(0, None)
            lo(l, base + 4)
            with dve.Fori(0, NF - 2) as f:
                lo(l, base + 5, f)
                product(f + 1, base + 3, f)
                lo(l, base + 6, f)
                split(f + 1, f)
                lo(l, base + 7, f)
            product(NF - 1, base + 3, NF - 2)
            split(NF - 1, NF - 2)
            lo(l, base + 3 * NF - 1)

        def split_x(pair, stage):
            part = slice(2 * pair, 2 * pair + 2)
            dve.tensor_copy(xhi[:, part, :], xf[:, part, :]).then_inc(x_hi, 1)
            dve.wait_ge(x_hi, stage * 4 + (pair + 1))
            dve.tensor_tensor(xlo[:, part, :], xf[:, part, :], xhi[:, part, :].bitcast(F32),
                              ALU.subtract).then_inc(x_ready, 1)

        def layer_norm(l, w, early):
            turn = l * 3 + w
            coef = ALPHA if w == 1 else 2 * ALPHA
            for k in early[:2]:
                lo(l, k)
            dve.wait_ge(xtok_ready, turn * 2 + 1)
            dve.wait_ge(x_loaded, 16)
            dve.wait_ge(w_used, done_no(l, MIX_BASE + U_MIX - 1 if w == 1 else FFN_BASE[w // 2] + U_FFN - 1))
            for t in range(TT):
                dve.scalar_tensor_tensor(out=z[:, t, :], in0=xtok[:, t, :], scalar=coef,
                                         in1=flat(ps[:, 2 * t:2 * t + 2, :]), op0=ALU.mult,
                                         op1=ALU.add).then_inc(ln_sum, 1)
                dve.wait_ge(ln_sum, turn * 2 + (t + 1))
                for c in range(2):
                    last = dve.bn_stats(stats[:, t, c, :], z[:, t, 512 * c:512 * c + 512])
                last.then_inc(ln_stats, 1)
                dve.wait_ge(ln_stats, turn * 2 + (t + 1))
                dve.memset(pause[:, :], 0.0)
                dve.bn_aggr(mv[:, t, :], flat(stats[:, t, :, :])).then_inc(ln_var, 1)
            for t in range(TT):
                dve.wait_ge(ln_std, turn * 2 + (t + 1))
                dve.reciprocal(rstd[:, t:t + 1], std[:, t:t + 1]).then_inc(ln_rstd, 1)
                dve.wait_ge(ln_rstd, turn * 2 + (t + 1))
                dve.tensor_scalar(z[:, t, :], z[:, t, :], mv[:, t, 0:1], rstd[:, t:t + 1],
                                  ALU.subtract, ALU.mult).then_inc(ln_rows, 1)
            for k in early[2:]:
                lo(l, k)
            dve.wait_ge(ln_turned, turn * 2 + 2)
            for k in range(4, 8):
                dve.tensor_scalar(xf[:, k, :], ps[:, 4 + k // 2, (k % 2) * SEQ:(k % 2 + 1) * SEQ],
                                  par_col("ln_g", 8 * w + k), par_col("ln_b", 8 * w + k),
                                  ALU.mult, ALU.add).then_inc(x_dve, 1)
            for pair in range(4):
                if pair < 2:
                    dve.wait_ge(x_act, turn * 4 + (2 * pair + 2))
                else:
                    dve.wait_ge(x_dve, turn * 4 + (2 * pair - 2))
                split_x(pair, turn + 1)

        def mixer(l):
            m0 = MIX_BASE

            def stt(out, in0, scalar, op0, in1, op1):
                return dve.scalar_tensor_tensor(out=out, in0=in0, scalar=scalar, in1=in1, op0=op0, op1=op1)

            def rotate(r, dst, cos, sin, n=2):
                def wide(x):
                    return halves(x[:, :]) if n == 2 else x[:, 0:SEQ]
                tables = [twice(t) if n == 2 else t[:, :] for t in (cos, sin)]
                dve.wait_ge(rot_copied, l * 6 + (r + 1))
                dve.tensor_tensor(wide(rot), wide(rot), tables[0], ALU.mult)
                dve.tensor_tensor(wide(rot_sw), wide(rot_sw), tables[1], ALU.mult).then_inc(rot_parts, 1)
                dve.wait_ge(rot_parts, l * 6 + (r + 1))
                dve.tensor_tensor(dst, wide(rot), wide(rot_sw), ALU.add).then_inc(rotated, 1)

            def conv(i):
                dve.wait_ge(conv_copied, l * 4 + (i + 1))
                dve.wait_ge(conv_pad, l + 1)
                for n, tap in enumerate(range(CONV - 1, -1, -1)):
                    for c, j in enumerate((2 * i, 2 * i + 1)):
                        col = par_col("conv_w", 8 * tap + j)
                        shifted = conv_in[:, j, tap:tap + SEQ]
                        if n == 0:
                            dve.tensor_scalar(ml_qk[:, j, :], shifted, col, par_col("conv_b", j),
                                              ALU.mult, ALU.add).then_inc(conv_tap, 1)
                        else:
                            dve.wait_ge(conv_tap, l * 32 + (8 * i + 2 * (n - 1) + c + 1))
                            stt(ml_qk[:, j, :], shifted, col, ALU.mult, ml_qk[:, j, :], ALU.add).then_inc(conv_tap, 1)

            def scores(h):
                dve.wait_ge(s_done, l * 4 + (h + 1))
                if h >= 2:
                    dve.wait_ge(p_turned, l * 4 + (h - 1))
                stt(sc[:, h % 2, :], ps[:, BANK[f"S{h}"], 0:384], MLA_SCALE, ALU.mult, C("mask"),
                    ALU.add).then_inc(s_masked, 1)
                dve.wait_ge(s_masked, l * 4 + (h + 1))
                for q, (c0, c1) in enumerate(((0, P), (P, 3 * P))):
                    last = dve.tensor_reduce(mx[:, h, q:q + 1], sc[:, h % 2, c0:c1], AX.X, ALU.max)
                last.then_inc(s_max, 1)
                dve.wait_ge(s_max, l * 4 + (h + 1))
                dve.tensor_scalar(mx[:, h, :], mx[:, h, :], -1.0, None, ALU.mult).then_inc(s_negmax, 1)

            def probs(h):
                dve.wait_ge(s_exp, l * 4 + (h + 1))
                dve.reciprocal(rinv[:, h, :], rowsum[:, h, :]).then_inc(s_rsum, 1)
                dve.wait_ge(s_rsum, l * 4 + (h + 1))
                for q, (c0, c1) in enumerate(((0, P), (P, 3 * P))):
                    last = dve.tensor_scalar(sc[:, h % 2, c0:c1], sc[:, h % 2, c0:c1], rinv[:, h, q:q + 1],
                                             None, ALU.mult)
                last.then_inc(s_probs, 1)

            def split_y(n, src):
                hi_p, lo_p = (flat(t[:, n // 2, 2 * (n % 2):2 * (n % 2) + 2, :]) for t in (yhi, ylo))
                dve.tensor_copy(hi_p, src).then_inc(y_hi, 1)
                dve.wait_ge(y_hi, l * 6 + (n + 1))
                dve.tensor_tensor(lo_p, src, hi_p.bitcast(F32), ALU.subtract).then_inc(y_lo, 1)

            def y_mla(p):
                dve.wait_ge(mla_done, l * 2 + (p + 1))
                split_y(p, ps[:, BANK[f"pv{p}"], :])

            def args(h):
                dve.wait_ge(bc_copied, l * 4 + (h + 1))
                dve.wait_ge(a_copied, l + 1)
                if h < 2:
                    dve.wait_ge(p_turned, l * 4 + (h + 3))
                else:
                    dve.wait_ge(ml_summed, l * 4 + (h - 1))
                stt(sc[:, h % 2, 0:SEQ], bc[:, h % 2, 0:SEQ], a_col[:, 0, h:h + 1], ALU.subtract,
                    C("pmask", SEQ), ALU.add)
                stt(sc[:, h % 2, SEQ:384], bc[:, h % 2, P:SEQ], a_col[:, 1, h:h + 1], ALU.subtract,
                    C("pmask", P, SEQ), ALU.add).then_inc(decay_arg, 1)

            def weigh(h):
                dve.wait_ge(ml_scored, l * 4 + (h + 1))
                dve.wait_ge(decay_ready, l * 4 + (h + 1))
                stt(sc[:, h % 2, :], ps[:, BANK[f"mS{h}"], 0:384], HEAD_SCALE, ALU.mult, sc[:, h % 2, :],
                    ALU.mult).then_inc(ml_probs, 1)

            def ml_out(h):
                bank = ps[:, BANK[f"mpv{h}"], :]
                floor = bc[:, h % 2, SEQ:]
                dve.wait_ge(ml_summed, l * 4 + (h + 1))
                stt(floor, bank[:, SEQ:], -1.0, ALU.mult, floor, ALU.max).then_inc(den_step, 1)
                dve.wait_ge(den_step, l * 12 + (3 * h + 1))
                dve.tensor_tensor(floor, bank[:, SEQ:], floor, ALU.max).then_inc(den_step, 1)
                dve.wait_ge(den_step, l * 12 + (3 * h + 2))
                dve.reciprocal(floor, floor).then_inc(den_step, 1)
                dve.wait_ge(den_step, l * 12 + (3 * h + 3))
                dve.tensor_tensor(ht[:, h // 2, (h % 2) * SEQ:(h % 2 + 1) * SEQ], bank[:, 0:SEQ], floor,
                                  ALU.mult).then_inc(h_ready, 1)

            def center(n):
                p = n % 2
                dve.wait_ge(h_means, l * 4 + (n + 1))
                stt(ht[:, p, :], ps[:, BANK[f"{'mr'[n // 2]}_mean{p}"], :], -1.0 / DH, ALU.mult, ht[:, p, :],
                    ALU.add).then_inc(h_centred, 1)
                dve.wait_ge(h_centred, l * 4 + (n + 1))
                if n:
                    dve.wait_ge(h_vars, l * 4 + n)
                dve.tensor_tensor(ht_sq[:, :], ht[:, p, :], ht[:, p, :], ALU.mult).then_inc(h_squared, 1)

            def normalise(n):
                p = n % 2
                dve.wait_ge(h_std, l * 4 + (n + 1))
                dve.reciprocal(ht_rs[:, :], ht_rs[:, :]).then_inc(h_rstd, 1)
                dve.wait_ge(h_rstd, l * 4 + (n + 1))
                for i in range(2):
                    part = slice(i * SEQ, (i + 1) * SEQ)
                    last = stt(ht[:, p, part], ht[:, p, part], par_col("ml_g" if n < 2 else "rt_g", 2 * p + i),
                               ALU.mult, ht_rs[:, part], ALU.mult)
                last.then_inc(h_scaled, 1)
                dve.wait_ge(mo_ready if n < 2 else rg_ready, l * 2 + (p + 1))
                dve.wait_ge(h_scaled, l * 4 + (n + 1))
                dve.tensor_tensor(ht[:, p, :], ht[:, p, :], flat((mo if n < 2 else rg)[:, 2 * p:2 * p + 2, :]),
                                  ALU.mult).then_inc(h_gated, 1)
                dve.wait_ge(h_gated, l * 4 + (n + 1))
                split_y(n + 2, ht[:, p, :])

            def ret_probs(h):
                dve.wait_ge(rt_scored, l * 4 + (h + 1))
                if h >= 2:
                    dve.wait_ge(rt_summed, l * 2 + 1)
                stt(pt[:, h % 2, :], ps[:, BANK[f"rS{h}"], 0:384], HEAD_SCALE, ALU.mult,
                    C("decay", 384, 384 * h), ALU.mult).then_inc(rt_probs, 1)

            def ret_out(p):
                dve.wait_ge(rt_summed, l * 2 + (p + 1))
                dve.wait_ge(y_lo, l * 6 + (p + 3))
                dve.tensor_copy(ht[:, p, :], ps[:, BANK[f"rpv{p}"], :]).then_inc(rt_copied, 1)

            dve.wait_ge(xtok_ready, l * 6 + 3)
            dve.memset(conv_in[:, :, 0:CONV - 1], 0.0).then_inc(conv_pad, 1)
            lo(l, m0 + 3)
            for i in range(3):
                part = slice(2 * i, min(2 * i + 2, QC + VC))
                dve.wait_ge(lat_copied, l * 3 + (i + 1))
                dve.tensor_tensor(lat_sq[:, part, :], lat[:, part, :], lat[:, part, :],
                                  ALU.mult).then_inc(lat_squared, 1)
                if i < 2:
                    lo(l, m0 + 4 + i)
            rotate(0, k_rope[:, :], cos_m, sin_m, 1)
            lo(l, m0 + 6)
            dve.wait_ge(lat_std, l + 1)
            dve.reciprocal(lat_rs[:, :], lat_rs[:, :]).then_inc(lat_rstd, 1)
            dve.wait_ge(lat_rstd, l + 1)
            for c in range(QC + VC):
                g = par_col("q_g", c) if c < QC else par_col("kv_g", c - QC)
                last = stt(lat[:, c, :], lat[:, c, :], g, ALU.mult,
                           lat_rs[:, 0:SEQ] if c < QC else lat_rs[:, SEQ:], ALU.mult)
            last.then_inc(lat_scaled, 1)
            dve.wait_ge(lat_scaled, l + 1)
            dve.tensor_copy(lhi[:, :, :], lat[:, :, :]).then_inc(lat_hi, 1)
            dve.wait_ge(lat_hi, l + 1)
            dve.tensor_tensor(llo[:, :, :], lat[:, :, :], lhi[:, :, :].bitcast(F32), ALU.subtract).then_inc(lat_lo, 1)
            for i in range(4):
                conv(i)
                lo(l, m0 + 7 + i)
            lo(l, m0 + 11)
            rotate(1, q_rope[:, :, :], cos_m, sin_m)
            lo(l, m0 + 12)
            dve.wait_ge(w_used, done_no(l, m0 + 9))
            for t in range(TT):
                dve.tensor_copy(v_mla[:, t, :], ps[:, BANK[f"v{t}"], :]).then_inc(v_copied, 1)
            lo(l, m0 + 13)
            dve.wait_ge(w_used, done_no(l, m0 + 11))
            for t in range(TT):
                dve.tensor_copy(ml_v[:, t, :], ps[:, BANK[f"mv{t}"], :]).then_inc(v_copied, 1)
            lo(l, m0 + 14)
            scores(0)
            scores(1)
            gbank = ps[0:HEADS, BANK["gates"], :]
            dve.wait_ge(w_used, done_no(l, m0 + 12))
            dve.tensor_scalar(row_i[:, :], gbank[:, 0:SEQ], par_col("i_b", 0)[0:HEADS, :], None, ALU.add)
            dve.tensor_scalar(row_f[:, :], gbank[:, SEQ:], par_col("f_b", 0)[0:HEADS, :], None,
                              ALU.add).then_inc(f_pre, 1)
            dve.wait_ge(f_pre, l + 1)
            stt(row_t[:, :], row_f[:, :], -1.0, ALU.mult, row_f[:, :], ALU.max).then_inc(f_abs, 1)
            probs(0)
            probs(1)
            lo(l, m0 + 15)
            dve.wait_ge(f_log, l + 1)
            dve.memset(row_m[:, SEQ:], 0.0)
            stt(row_f[:, :], row_f[:, :], 0.0, ALU.min, row_t[:, :], ALU.subtract).then_inc(log_f, 1)
            dve.wait_ge(log_f, l + 1)
            dve.tensor_tensor_scan(row_t[:, :], row_f[:, :], row_m[:, SEQ:], 0.0, ALU.add,
                                   ALU.add).then_inc(g_row_ready, 1)
            dve.wait_ge(g_row_ready, l + 1)
            dve.tensor_tensor(row_i[:, :], row_i[:, :], row_t[:, :], ALU.subtract).then_inc(a_row_ready, 1)
            dve.wait_ge(a_row_ready, l + 1)
            dve.tensor_tensor_scan(row_m[:, 0:SEQ], row_i[:, :], row_i[:, :], 0.0, ALU.max,
                                   ALU.max).then_inc(m_row_ready, 1)
            dve.wait_ge(m_row_ready, l + 1)
            dve.tensor_tensor(row_t[:, :], row_t[:, :], row_m[:, 0:SEQ], ALU.add).then_inc(gm_row_ready, 1)
            lo(l, m0 + 16)
            y_mla(0)
            scores(2)
            scores(3)
            dve.wait_ge(a_turned, l + 1)
            dve.tensor_copy(flat(a_col[:, :, :]), ps[:, BANK["aT"], 0:TT * HEADS]).then_inc(a_copied, 1)
            probs(2)
            probs(3)
            rotate(2, rq[:, 0:2, :], cos_r, sin_r)
            lo(l, m0 + 17)
            rotate(3, rq[:, 2:4, :], cos_r, sin_r)
            lo(l, m0 + 18)
            args(0)
            args(1)
            y_mla(1)
            weigh(0)
            weigh(1)
            rotate(4, rk[:, 0:2, :], cos_r, sin_r)
            lo(l, m0 + 19)
            ml_out(0)
            ml_out(1)
            rotate(5, rk[:, 2:4, :], cos_r, sin_r)
            lo(l, m0 + 20)
            center(0)
            args(2)
            args(3)
            weigh(2)
            weigh(3)
            dve.wait_ge(w_used, done_no(l, m0 + 18))
            for t in range(TT):
                dve.tensor_copy(rv[:, t, :], ps[:, BANK[f"rv{t}"], :]).then_inc(v_copied, 1)
            lo(l, m0 + 21)
            ml_out(2)
            ml_out(3)
            ret_probs(0)
            ret_probs(1)
            lo(l, m0 + 22)
            normalise(0)
            center(1)
            ret_out(0)
            ret_probs(2)
            ret_probs(3)
            lo(l, m0 + 23)
            center(2)
            lo(l, m0 + 24)
            normalise(1)
            ret_out(1)
            lo(l, m0 + 25)
            center(3)
            normalise(2)
            dve.memset(merged[:, :, :], 0.0).then_inc(merge_zero, 1)
            normalise(3)

            with dve.Fori(0, 3) as b:
                turn = l * 3 + b
                for h in range(2):
                    for i in range(3):
                        lo(l, m0 + 26 + 3 * h + i, b * 2)
                    dve.wait_ge(w_used, done_no(l, m0 + 25 + 3 * h, b * 2))
                    dve.wait_ge(gates_ready, turn * 4 + (2 * h + 3))
                    for c in range(2):
                        part = gate[:, 2 * c:2 * c + 2, :]
                        dve.tensor_tensor(part, halves(ps[:, 6 + c, :]), part, ALU.mult).then_inc(gate_used, 1)
                    dve.wait_ge(merge_zero, l + 1)
                    for c in range(2):
                        dst = merged[:, 4 * h + 2 * c:4 * h + 2 * c + 2, :]
                        dve.wait_ge(gate_used, turn * 4 + (2 * h + c + 1))
                        dve.tensor_tensor(dst, dst, gate[:, 2 * c:2 * c + 2, :], ALU.add).then_inc(branch_added, 1)
            dve.wait_ge(branch_added, l * 12 + 13)
            for i in range(4):
                part = slice(2 * i, 2 * i + 2)
                dve.tensor_copy(mhi[:, part, :], merged[:, part, :]).then_inc(m_hi, 1)
                dve.wait_ge(m_hi, l * 4 + (i + 1))
                dve.tensor_tensor(mlo[:, part, :], merged[:, part, :], mhi[:, part, :].bitcast(F32),
                                  ALU.subtract).then_inc(m_lo, 1)
            lo(l, m0 + 44)

        def after_step(n):
            dve.wait_ge(angle_step, n)

        dve.wait_ge(const_loaded, 48)
        dve.tensor_copy(pos_f[:, :], pos_i[:, :]).then_inc(angle_step, 1)
        for n, table in enumerate((cos_r, sin_r, cos_m, sin_m)):
            quarter = 0.25 if n % 2 == 0 else 0.0
            s0 = ANGLE_STEPS * n + 1
            after_step(s0)
            dve.tensor_scalar(ang[:, :], pos_f[:, :], C("invf", 1, n // 2), None, ALU.mult).then_inc(angle_step, 1)
            after_step(s0 + 1)
            dve.tensor_scalar(turns[:, :], ang[:, :], 1 / TWO_PI, quarter, ALU.mult, ALU.add).then_inc(angle_step, 1)
            after_step(s0 + 2)
            dve.tensor_scalar(turns[:, :], turns[:, :], ROUND, None, ALU.add).then_inc(angle_step, 1)
            after_step(s0 + 3)
            dve.tensor_scalar(turns[:, :], turns[:, :], ROUND, None, ALU.subtract).then_inc(angle_step, 1)
            for i, part in enumerate((PI_A, PI_B, PI_C)):
                after_step(s0 + 4 + i)
                dve.scalar_tensor_tensor(out=ang[:, :], in0=turns[:, :], scalar=-part, in1=ang[:, :],
                                         op0=ALU.mult, op1=ALU.add).then_inc(angle_step, 1)
            after_step(s0 + 7)
            dve.tensor_scalar(ang[:, :], ang[:, :], quarter * TWO_PI, None, ALU.add).then_inc(angle_step, 1)
            after_step(s0 + 8)
            dve.tensor_scalar(table[:, :], ang[:, :], PI_MAX, -PI_MAX, ALU.min, ALU.max).then_inc(angle_step, 1)
        for n, table in ((1, sin_r), (3, sin_m)):
            dve.wait_ge(sin_ready, n + 1)
            dve.tensor_scalar(table[:, :], table[:, :], C("sign", 1, n // 2), None, ALU.mult).then_inc(sign_ready, 1)
        dve.wait_ge(sign_ready, 2)
        for pair in range(4):
            dve.wait_ge(x_copied, pair + 1)
            split_x(pair, 0)

        with dve.Fori(0, DEPTH) as l:
            dve.tensor_copy(par[:, :], par_all[:, bass.ds(l, 1), :].rearrange("p a b -> p (a b)")).then_inc(par_ready, 1)
            dve.wait_ge(par_ready, l + 1)
            ffn(l, 0)
            layer_norm(l, 0, [MIX_BASE, MIX_BASE + 1, MIX_BASE + 2])
            mixer(l)
            layer_norm(l, 1, [FFN_BASE[1], FFN_BASE[1] + 1])
            ffn(l, 1)
            layer_norm(l, 2, [])

    @block.tensor
    def _(pe):
        def tile3(out, w_hi_ap, w_lo_ap, x_hi_ap, x_lo_ap, start, stop):
            pe.matmul(out, w_hi_ap, x_hi_ap, start=start, stop=False)
            pe.matmul(out, w_hi_ap, x_lo_ap, start=False, stop=False)
            return pe.matmul(out, w_lo_ap, x_hi_ap, start=False, stop=stop)

        def slot(k, width):
            n = size_of(k)
            return tuple(t[:, k % RING, 0:n].rearrange("p (k n) -> p k n", n=width) for t in (whi, wlo))

        def features(out, k, width, cols, xh, xl, n_k):
            wh, wl = slot(k, width)
            for kk in range(n_k):
                last = tile3(out, wh[:, kk, cols], wl[:, kk, cols], xh(kk), xl(kk), kk == 0, kk == n_k - 1)
            return last

        def x_h(kk):
            return xhi[:, kk, :]

        def x_l(kk):
            return xlo[:, kk, :]

        def two_chunks(bank, k, width=256, n_k=KC, xh=x_h, xl=x_l):
            for c in range(2):
                last = features(ps[:, bank, c * SEQ:(c + 1) * SEQ], k, width, slice(c * P, (c + 1) * P), xh, xl, n_k)
            return last

        def tokens(k, kk, t_hi, t_lo, banks):
            wh, wl = slot(k, D_MODEL)
            for n, (bank, start, stop) in enumerate(banks):
                cols = slice(512 * n, 512 * n + 512)
                for i, (s, w) in enumerate(((t_hi, wh), (t_hi, wl), (t_lo, wh))):
                    last = pe.matmul(ps[:, bank, :], s, w[:, kk, cols], start=start and i == 0,
                                     stop=stop and i == 2, skip_group_check=True)
            return last

        def ffn(l, w):
            base = FFN_BASE[w]

            def gate_of(j, k, f):
                pe.wait_ge(w_lo, done_no(l, k, f))
                if j is not None:
                    pe.wait_ge(silu_done, step_no(l, w, j) - 1)
                two_chunks(4, k).then_inc(w_used, 1)

            def up_of(j, k, f):
                pe.wait_ge(w_lo, done_no(l, k, f))
                if j is not None:
                    pe.wait_ge(prod_done, step_no(l, w, j))
                two_chunks(5, k).then_inc(w_used, 1)

            def down_of(j, k, f):
                pe.wait_ge(w_lo, done_no(l, k, f))
                pe.wait_ge(y_cleared, l * 2 + (w + 1))
                pe.wait_ge(hid_lo, step_no(l, w, j) + 1)
                for kk in range(2):
                    for t in range(TT):
                        rows = slice(kk * SEQ + t * P, kk * SEQ + (t + 1) * P)
                        last = tokens(k, kk, hhi[:, rows], hlo[:, rows], [(2 * t, False, True), (2 * t + 1, False, True)])
                last.then_inc(w_used, 1)

            pe.wait_ge(x_ready, l * 12 + (8 * w + 4))
            gate_of(None, base, 0)
            up_of(None, base + 1, 0)
            with pe.Fori(0, NF - 1) as f:
                gate_of(f + 1, base + 2, f)
                up_of(f + 1, base + 3, f)
                down_of(f, base + 4, f)
            down_of(NF - 1, base + 3 * NF - 1, 0)

        def layer_norm(l, w):
            for t in range(TT):
                pe.wait_ge(ln_rows, l * 6 + (2 * w + t + 1))
                for k in range(KC):
                    last = pe.transpose(ps[:, 4 + k // 2, (k % 2) * SEQ + t * P:(k % 2) * SEQ + (t + 1) * P],
                                        z[:, t, k * P:(k + 1) * P], ident)
                last.then_inc(ln_turned, 1)

        def mixer(l):
            m0 = MIX_BASE

            def project(m, job):
                pe.wait_ge(w_lo, done_no(l, m0 + m))
                two_chunks(BANK[job], m0 + m).then_inc(w_used, 1)

            def half_tokens(m, jobs, cols):
                pe.wait_ge(w_lo, done_no(l, m0 + m))
                wh, wl = slot(m0 + m, 256)
                for t, job in enumerate(jobs):
                    tok = slice(t * P, (t + 1) * P)
                    for kk in range(KC):
                        last = tile3(ps[:, BANK[job], cols:cols + 256], xhi[:, kk, tok], xlo[:, kk, tok],
                                     wh[:, kk, :], wl[:, kk, :], kk == 0, kk == KC - 1)
                last.then_inc(w_used, 1)

            def latent(off):
                return (lambda kk: lhi[:, off + kk, :]), (lambda kk: llo[:, off + kk, :])

            def mla_scores(h):
                r = slice(64 * (h % 2), 64 * (h % 2) + 64)
                out = ps[:, BANK[f"S{h}"], :]
                for q, (lo_c, hi_c, n) in enumerate(((0, P, P), (P, 3 * P, SEQ))):
                    tok = slice(q * P, (q + 1) * P)
                    pe.matmul(out[:, lo_c:hi_c], q_nope[:, h, tok], k_nope[:, h, 0:n], start=True, stop=False)
                    last = pe.matmul(out[:, lo_c:hi_c], q_rope[r, h // 2, tok], k_rope[r, 0:n], start=False, stop=True)
                last.then_inc(s_done, 1)

            def mla_turn(h):
                pe.wait_ge(s_probs, l * 4 + (h + 1))
                for src in range(3):
                    last = pe.transpose(ps[:, BANK[f"T{h}"], src * P:(src + 1) * P],
                                        sc[:, h % 2, src * P:(src + 1) * P], ident)
                last.then_inc(p_turned, 1)

            def values(out, v, h, probs):
                cols = slice(h * DH, (h + 1) * DH)
                pe.matmul(out[:, 0:SEQ], v[:, 0, cols], probs[:, 0:SEQ], start=True, stop=False)
                return pe.matmul(out[:, P:SEQ], v[:, 1, cols], probs[:, SEQ:384], start=False, stop=True)

            def mla_values(p):
                for i in range(2):
                    pe.wait_ge(p_copied, l * 4 + (2 * p + i + 1))
                    last = values(ps[:, BANK[f"pv{p}"], i * SEQ:(i + 1) * SEQ], v_mla, 2 * p + i, pt[:, i, :])
                last.then_inc(mla_done, 1)

            def ret_values(p):
                for i in range(2):
                    pe.wait_ge(rt_probs, l * 4 + (2 * p + i + 1))
                    last = values(ps[:, BANK[f"rpv{p}"], i * SEQ:(i + 1) * SEQ], rv, 2 * p + i, pt[:, i, :])
                last.then_inc(rt_summed, 1)

            def key_scores(job, q, k, h):
                out = ps[:, BANK[job], :]
                pe.matmul(out[:, 0:SEQ], k[:, h, 0:P], q[:, h, :], start=True, stop=True)
                return pe.matmul(out[:, SEQ:384], k[:, h, P:SEQ], q[:, h, P:SEQ], start=True, stop=True)

            def ml_scores(h):
                key_scores(f"mS{h}", ml_qk[:, 0:4, :], ml_qk[:, 4:8, :], h).then_inc(ml_scored, 1)

            def ret_scores(h):
                key_scores(f"rS{h}", rq, rk, h).then_inc(rt_scored, 1)

            def ml_values(h):
                out, weights = ps[:, BANK[f"mpv{h}"], :], sc[:, h % 2, :]
                pe.wait_ge(ml_probs, l * 4 + (h + 1))
                values(out[:, 0:SEQ], ml_v, h, weights)
                pe.matmul(out[:, SEQ:], ones, weights[:, 0:SEQ], start=True, stop=False)
                pe.matmul(out[:, SEQ + P:], ones, weights[:, SEQ:384], start=False, stop=True).then_inc(ml_summed, 1)

            def spread(h):
                pe.matmul(ps[:, BANK[f"bc{h}"], :], C("sel", P, h * P)[0:HEADS, :], row_m[:, :],
                          start=True, stop=True).then_inc(bc_done, 1)

            def means(n):
                pe.matmul(ps[:, BANK[f"{'mr'[n // 2]}_mean{n % 2}"], :], ones, ht[:, n % 2, :],
                          start=True, stop=True).then_inc(h_means, 1)

            def variances(n):
                pe.wait_ge(h_squared, l * 4 + (n + 1))
                pe.matmul(ps[:, BANK[f"{'mr'[n // 2]}_var{n % 2}"], :], ones, ht_sq[:, :],
                          start=True, stop=True).then_inc(h_vars, 1)

            pe.wait_ge(x_ready, l * 12 + 8)
            project(0, "c0")
            project(1, "c1")
            pe.wait_ge(w_lo, done_no(l, m0 + 2))
            features(ps[:, BANK["c2"], 0:SEQ], m0 + 2, 192, slice(0, P), x_h, x_l, KC)
            last = features(ps[0:ROPE, BANK["c2"], SEQ:], m0 + 2, 192, slice(P, 192), x_h, x_l, KC)
            last.then_inc(w_used, 1)
            project(3, "qk0")
            pe.wait_ge(lat_squared, l * 3 + 3)
            for c in range(QC):
                pe.matmul(ps[:, BANK["rms"], 0:SEQ], ones, lat_sq[:, c, :], start=c == 0, stop=c == QC - 1)
            for c in range(QC, QC + VC):
                last = pe.matmul(ps[:, BANK["rms"], SEQ:], ones, lat_sq[:, c, :], start=c == QC,
                                 stop=c == QC + VC - 1)
            last.then_inc(lat_summed, 1)
            pe.wait_ge(lat_copied, l * 3 + 1)
            project(4, "qk1")
            pe.wait_ge(lat_copied, l * 3 + 2)
            project(5, "qk2")
            pe.wait_ge(rot_copied, l * 6 + 1)
            project(6, "qk3")

            pe.wait_ge(lat_lo, l + 1)
            q_h, q_l = latent(0)
            for i in range(2):
                k = m0 + 7 + i
                pe.wait_ge(w_lo, done_no(l, k))
                if i == 0:
                    pe.wait_ge(conv_copied, l * 4 + 2)
                else:
                    pe.wait_ge(conv_copied, l * 4 + 3)
                two_chunks(BANK[f"qn{i}"], k, 384, QC, q_h, q_l)
                features(ps[:, BANK["qr"], i * SEQ:(i + 1) * SEQ], k, 384, slice(2 * P, 3 * P), q_h, q_l, QC)\
                    .then_inc(w_used, 1)
            k = m0 + 9
            k_h, k_l = latent(QC)
            pe.wait_ge(w_lo, done_no(l, k))
            for i in range(2):
                if i == 0:
                    pe.wait_ge(conv_copied, l * 4 + 4)
                else:
                    pe.wait_ge(q_copied, l * 2 + 1)
                for c in range(2):
                    features(ps[:, BANK[f"kn{i}"], c * SEQ:(c + 1) * SEQ], k, 1024,
                             slice(256 * (2 * i + c), 256 * (2 * i + c) + P), k_h, k_l, VC)
            wv = [t[:, k % RING, 0:VC * 1024].rearrange("p (k h n) -> p k h n", h=HEADS, n=256) for t in (whi, wlo)]
            for t in range(TT):
                if t == 0:
                    pe.wait_ge(rot_copied, l * 6 + 2)
                else:
                    pe.wait_ge(q_copied, l * 2 + 2)
                tok = slice(t * P, (t + 1) * P)
                for kk in range(VC):
                    last = tile3(ps[:, BANK[f"v{t}"], :], lhi[:, QC + kk, tok], llo[:, QC + kk, tok],
                                 wv[0][:, kk, :, P:256], wv[1][:, kk, :, P:256], kk == 0, kk == VC - 1)
            last.then_inc(w_used, 1)
            pe.wait_ge(k_copied, l * 2 + 2)
            half_tokens(10, ("mv0", "mv1"), 0)
            half_tokens(11, ("mv0", "mv1"), 256)
            pe.wait_ge(w_lo, done_no(l, m0 + 12))
            pe.wait_ge(v_copied, l * 6 + 1)
            for i in range(2):
                last = features(ps[0:HEADS, BANK["gates"], i * SEQ:(i + 1) * SEQ], m0 + 12, 2 * HEADS,
                                slice(i * HEADS, (i + 1) * HEADS), x_h, x_l, KC)
            last.then_inc(w_used, 1)

            pe.wait_ge(rotated, l * 6 + 2)
            mla_scores(0)
            mla_scores(1)
            pe.wait_ge(v_copied, l * 6 + 2)
            project(13, "rq0")
            mla_turn(0)
            pe.wait_ge(lat_std, l + 1)
            mla_turn(1)
            pe.wait_ge(v_copied, l * 6 + 3)
            project(14, "rq1")
            pe.wait_ge(s_masked, l * 4 + 1)
            mla_values(0)
            pe.wait_ge(s_masked, l * 4 + 2)
            mla_scores(2)
            pe.wait_ge(p_copied, l * 4 + 1)
            mla_scores(3)
            pe.wait_ge(p_copied, l * 4 + 2)
            pe.wait_ge(a_row_ready, l + 1)
            for t in range(TT):
                last = pe.matmul(ps[:, BANK["aT"], t * HEADS:(t + 1) * HEADS], row_i[:, t * P:(t + 1) * P],
                                 ident[0:HEADS, 0:HEADS], start=True, stop=True)
            last.then_inc(a_turned, 1)
            pe.wait_ge(v_copied, l * 6 + 4)
            project(15, "rk0")
            pe.wait_ge(y_lo, l * 6 + 1)
            mla_turn(2)
            pe.wait_ge(s_masked, l * 4 + 3)
            mla_turn(3)
            pe.wait_ge(floor_ready, l + 1)
            pe.wait_ge(s_masked, l * 4 + 4)
            spread(0)
            pe.wait_ge(a_copied, l + 1)
            spread(1)
            pe.wait_ge(f_pre, l + 1)
            project(16, "rk1")
            pe.wait_ge(p_copied, l * 4 + 3)
            mla_values(1)
            pe.wait_ge(qk_silu, l * 2 + 2)
            pe.wait_ge(p_copied, l * 4 + 4)
            ml_scores(0)
            pe.wait_ge(bc_copied, l * 4 + 1)
            ml_scores(1)
            pe.wait_ge(rot_copied, l * 6 + 4)
            half_tokens(17, ("rv0", "rv1"), 0)
            pe.wait_ge(bc_copied, l * 4 + 2)
            ml_values(0)
            pe.wait_ge(y_lo, l * 6 + 2)
            ml_values(1)
            pe.wait_ge(ml_probs, l * 4 + 2)
            spread(2)
            spread(3)
            half_tokens(18, ("rv0", "rv1"), 256)
            pe.wait_ge(h_ready, l * 4 + 2)
            means(0)
            ml_scores(2)
            pe.wait_ge(bc_copied, l * 4 + 3)
            ml_scores(3)
            pe.wait_ge(rot_copied, l * 6 + 5)
            project(19, "mo0")
            pe.wait_ge(bc_copied, l * 4 + 4)
            variances(0)
            pe.wait_ge(h_centred, l * 4 + 1)
            ml_values(2)
            pe.wait_ge(ml_probs, l * 4 + 3)
            ml_values(3)
            pe.wait_ge(rotated, l * 6 + 6)
            pe.wait_ge(ml_probs, l * 4 + 4)
            ret_scores(0)
            pe.wait_ge(h_std, l * 4 + 1)
            ret_scores(1)
            pe.wait_ge(rot_copied, l * 6 + 6)
            project(20, "mo1")
            pe.wait_ge(h_ready, l * 4 + 4)
            means(1)
            pe.wait_ge(v_copied, l * 6 + 6)
            ret_values(0)
            ret_scores(2)
            ret_scores(3)
            project(21, "rg0")
            pe.wait_ge(h_centred, l * 4 + 2)
            variances(1)
            pe.wait_ge(rt_copied, l * 2 + 1)
            means(2)
            pe.wait_ge(rt_probs, l * 4 + 3)
            ret_values(1)
            project(22, "rg1")
            pe.wait_ge(rt_probs, l * 4 + 4)
            variances(2)
            pe.wait_ge(h_std, l * 4 + 2)
            pe.wait_ge(rt_copied, l * 2 + 2)
            means(3)
            pe.wait_ge(h_centred, l * 4 + 3)
            variances(3)

            with pe.Fori(0, 3) as b:
                turn = l * 3 + b

                def y_h(kk):
                    return yhi[:, bass.ds(b, 1), kk, :].rearrange("p a n -> p (a n)")

                def y_l(kk):
                    return ylo[:, bass.ds(b, 1), kk, :].rearrange("p a n -> p (a n)")

                for h in range(2):
                    for i in range(2):
                        k = m0 + 23 + 3 * h + i
                        pe.wait_ge(w_lo, done_no(l, k, b * 2))
                        pe.wait_ge(gates_ready, turn * 4 + (2 + i if h else 1))
                        if not h:
                            pe.wait_ge(rg_ready, l * 2 + 2)
                        two_chunks(4 + i, k).then_inc(w_used, 1)
                    k = m0 + 25 + 3 * h
                    pe.wait_ge(w_lo, done_no(l, k, b * 2))
                    if h:
                        pe.wait_ge(gate_used, turn * 4 + 2)
                    else:
                        pe.wait_ge(branch_added, turn * 4 + 1)
                        pe.wait_ge(y_lo, l * 6 + 6)
                    for c in range(4):
                        last = features(ps[:, 6 + c // 2, (c % 2) * SEQ:(c % 2 + 1) * SEQ], k, 512,
                                        slice(c * P, (c + 1) * P), y_h, y_l, HEADS)
                    last.then_inc(w_used, 1)
            for i in range(MIX_OUT):
                k = m0 + 41 + i
                pe.wait_ge(w_lo, done_no(l, k))
                pe.wait_ge(m_lo, l * 4 + (i + 1))
                for kk in range(2):
                    chunk = 2 * i + kk
                    for t in range(TT):
                        tok = slice(t * P, (t + 1) * P)
                        ends = (chunk == 0, chunk == KC - 1)
                        last = tokens(k, kk, mhi[:, chunk, tok], mlo[:, chunk, tok],
                                      [(2 * t, *ends), (2 * t + 1, *ends)])
                last.then_inc(w_used, 1)

        pe.wait_ge(x_loaded, 16)
        pe.wait_ge(const_loaded, 48)
        for t in range(TT):
            for k in range(KC):
                last = pe.transpose(ps[:, 4 + k // 2, (k % 2) * SEQ + t * P:(k % 2) * SEQ + (t + 1) * P],
                                    xtok[:, t, k * P:(k + 1) * P], ident)
        last.then_inc(x_turned, 1)

        with pe.Fori(0, DEPTH) as l:
            ffn(l, 0)
            layer_norm(l, 0)
            mixer(l)
            layer_norm(l, 1)
            ffn(l, 1)
            layer_norm(l, 2)

    ctx.close()


def lay_out(inputs):
    a = {n: np.ascontiguousarray(inputs[n]) for n in (
        "x", "positions", "w_in", "mla_w_ukv", "w_out",
        "ffn1_w_gate", "ffn1_w_up", "ffn1_w_down", "ffn2_w_gate", "ffn2_w_up", "ffn2_w_down")}
    a["w_br"] = np.stack([np.asarray(inputs[f"w_br_{n}"]) for n in ("mla", "mlstm", "ret")], axis=1)
    uq = np.asarray(inputs["mla_w_uq"]).reshape(DEPTH, Q_LORA, 2, 2, DH + ROPE)
    a["mla_w_uq"] = np.concatenate([uq[..., :DH].reshape(DEPTH, Q_LORA, 2, 2 * DH),
                                    uq[..., DH:].reshape(DEPTH, Q_LORA, 2, 2 * ROPE)], axis=3)\
        .reshape(DEPTH, Q_LORA, -1)
    ln = [[np.asarray(inputs[f"ln{i}_{c}"]) for c in "gb"] for i in (1, 2, 3)]
    a["ln_rows"] = np.stack([np.stack(pair, axis=1) for pair in ln], axis=1)

    def columns(v):
        return np.asarray(v).reshape(DEPTH, -1, P).transpose(0, 2, 1)

    def rows_as_column(v):
        out = np.zeros((DEPTH, P, 1), np.float32)
        out[:, :HEADS, 0] = v
        return out

    gate_b = np.asarray(inputs["mlstm_gate_b"])
    parts = dict(
        ln_g=columns(np.concatenate([g for g, _ in ln], axis=1)),
        ln_b=columns(np.concatenate([b for _, b in ln], axis=1)),
        q_g=columns(inputs["mla_q_norm_g"]), kv_g=columns(inputs["mla_kv_norm_g"]),
        conv_w=columns(np.asarray(inputs["mlstm_conv_w"]).reshape(DEPTH, -1)),
        conv_b=columns(inputs["mlstm_conv_b"]),
        ml_g=columns(inputs["mlstm_norm_g"]), rt_g=columns(inputs["ret_norm_g"]),
        gate_b=columns(np.asarray(inputs["gate_b"]).reshape(DEPTH, -1)),
        i_b=rows_as_column(gate_b[:, :HEADS]), f_b=rows_as_column(gate_b[:, HEADS:]))
    assert all(parts[n].shape[2] == s for n, s in PARAM_SIZES.items())
    a["params"] = np.concatenate([parts[n] for n in PARAM_SIZES], axis=2)
    a["consts"] = constants()
    return {n: np.ascontiguousarray(v) for n, v in a.items()}


def kernel(**inputs):
    import concourse.bacc as bacc
    from concourse.bass_utils import run_bass_kernel_spmd

    arrays = lay_out(inputs)
    nc = bacc.Bacc("TRN2", target_bir_lowering=False, num_devices=1)
    a = {n: nc.dram_tensor(n, v.shape, mybir.dt.from_np(v.dtype), kind="ExternalInput").ap()
         for n, v in arrays.items()}
    a["out"] = nc.dram_tensor("out", (1, SEQ, D_MODEL), F32, kind="ExternalOutput").ap()
    build(nc, a)
    r = run_bass_kernel_spmd(nc, [arrays], core_ids=[0])
    return r.results[0]["out"]
```

```python
from contextlib import ExitStack

import concourse.bass as bass
import numpy as np
from concourse import mybir

F32 = mybir.dt.float32
F32R = mybir.dt.float32r
I32 = mybir.dt.int32
ALU = mybir.AluOpType
ACT = mybir.ActivationFunctionType
AX = mybir.AxisListType

P = 128
DEPTH, SEQ, D_MODEL, D_FF = 2, 256, 1024, 2816
TT = SEQ // P
KC = D_MODEL // P
HEADS, DH = 4, 128
ROPE = 64
Q_LORA, KV_LORA = 384, 256
QC, VC = Q_LORA // P, KV_LORA // P
CONV = 4
EPS = 1e-5
ALPHA = (2 * DEPTH) ** 0.25
MLA_SCALE = (DH + ROPE) ** -0.5
HEAD_SCALE = DH ** -0.5
NEG = -1e30
THETA = 10000.0

FB = 256
NF = D_FF // FB
UNIT = 2048
RING = 3
U_FFN = 3 * NF
MIX_FIXED, MIX_LOOP, MIX_OUT = 23, 18, 4
U_MIX = MIX_FIXED + MIX_LOOP + MIX_OUT
U_LAYER = 2 * U_FFN + U_MIX
FFN_BASE = (0, U_FFN + U_MIX)
MIX_BASE = U_FFN
assert U_LAYER % RING == 0 and U_FFN % RING == 0 and U_MIX % RING == 0

C_MQ, C_MV, C_GATES, C_MO = 704, 1728, 2240, 2248
C_RQ, C_RK, C_RV, C_RG, C_GL = 2760, 3272, 3784, 4296, 4808

PARAM_SIZES = dict(ln_g=24, ln_b=24, q_g=QC, kv_g=VC, conv_w=CONV * 8, conv_b=8, ml_g=4, rt_g=4,
                   gate_b=24, i_b=1, f_b=1)
PARAM_AT, NPAR = {}, 0
for _name, _n in PARAM_SIZES.items():
    PARAM_AT[_name] = NPAR
    NPAR += _n

CONST_SIZES = dict(ident=P, ones=P, mask=384, pmask=384, decay=HEADS * 384, sel=HEADS * P,
                   invf=2, sign=2, eps=2, one=1)
CONST_AT, NCONST = {}, 0
for _name, _n in CONST_SIZES.items():
    CONST_AT[_name] = NCONST
    NCONST += _n

TWO_PI = 2 * np.pi
PI_A = float(np.float32(6.28125))
PI_B = float(np.float32(np.round((TWO_PI - PI_A) * 2 ** 19) / 2 ** 19))
PI_C = float(np.float32(TWO_PI - PI_A - PI_B))
PI_MAX = 3.1415925
ANGLE_STEPS = 12
ROUND = 1.5 * 2.0 ** 23


def constants():
    c = np.zeros((P, NCONST), np.float32)
    at = CONST_AT
    i = np.arange(P)
    c[:, at["ident"]:at["ident"] + P] = np.eye(P)
    c[:, at["ones"]:at["ones"] + P] = 1.0
    lower = np.where(i[None, :] <= i[:, None], 0.0, NEG)
    c[:, at["mask"]:at["mask"] + 128] = lower
    c[:, at["mask"] + 256:at["mask"] + 384] = lower
    upper = np.where(i[None, :] >= i[:, None], 0.0, -NEG)
    c[:, at["pmask"]:at["pmask"] + 128] = upper
    c[:, at["pmask"] + 256:at["pmask"] + 384] = upper
    for h in range(HEADS):
        lg = np.log(1.0 - 2.0 ** (-5.0 - h))
        d = (i[None, :] - i[:, None]).astype(np.float64)
        o = at["decay"] + 384 * h
        c[:, o:o + 128] = c[:, o + 256:o + 384] = np.where(d >= 0, np.exp(lg * d), 0.0)
        c[:, o + 128:o + 256] = np.exp(lg * (d + 128))
        c[h, at["sel"] + h * P:at["sel"] + (h + 1) * P] = 1.0
    for n, half in enumerate((DH // 2, ROPE // 2)):
        c[:, at["invf"] + n] = np.float32(THETA) ** (-(i % half).astype(np.float32) / np.float32(half))
        c[:, at["sign"] + n] = np.where(i % (2 * half) < half, -1.0, 1.0)
    c[:, at["eps"]] = EPS
    c[:, at["eps"] + 1] = EPS / 0.25
    c[:, at["one"]] = 1.0
    return c


def build(nc, a):
    ctx = ExitStack()
    at = [nc.sbuf_base + 31 & ~31]

    def place(name, shape, dt, offset):
        return nc.alloc_sbuf_tensor_at(name, shape, dt, offset=offset)

    def sb(name, shape, dt=F32):
        t = place(name, shape, dt, at[0])
        at[0] += 4 * int(np.prod(shape[1:])) + 31 & ~31
        return t

    def region(nbytes):
        start = at[0]
        at[0] += nbytes
        return start

    def sem(name):
        return ctx.enter_context(nc.semaphore(name))

    cst = sb("cst", [P, NCONST])
    par_all = sb("par_all", [P, DEPTH, NPAR])
    par = sb("par", [P, NPAR])
    angles = sb("angles", [P, 4, SEQ])
    tables = sb("tables", [P, 4, SEQ])
    cos_r, sin_r, cos_m, sin_m = (tables[:, n, :] for n in range(4))
    raw = sb("raw", [P, RING, UNIT])
    whi, wlo = sb("whi", [P, RING, UNIT], F32R), sb("wlo", [P, RING, UNIT], F32R)
    xhi, xlo = sb("xhi", [P, KC, SEQ], F32R), sb("xlo", [P, KC, SEQ], F32R)
    xtok = sb("xtok", [P, TT, D_MODEL])
    stats = sb("stats", [P, TT, 2, 6])
    mv = sb("mv", [P, TT, 2])
    std = sb("std", [P, TT])
    rstd = sb("rstd", [P, TT])
    shift = sb("shift", [P, 1])
    mx = sb("mx", [P, HEADS, 2])
    rowsum = sb("rowsum", [P, HEADS, 2])
    rinv = sb("rinv", [P, HEADS, 2])
    a_col = sb("a_col", [P, TT, HEADS])
    pause, warm = sb("pause", [P, 1]), sb("warm", [P, 1])

    r_u2, r_rows, r_y, r_b = region(24576), region(5120), region(24576), region(15360)
    r_qk, r_mv, r_rq, r_rk = region(8192), region(4096), region(4096), region(4096)
    assert at[0] <= nc.sbuf_top, (at[0], nc.sbuf_top)
    silu = place("silu", [P, 2 * SEQ], F32, r_u2)
    hid = place("hid", [P, 2 * SEQ], F32, r_u2 + 2048)
    hhi = place("hhi", [P, 2 * SEQ], F32R, r_u2 + 4096)
    hlo = place("hlo", [P, 2 * SEQ], F32R, r_u2 + 6144)
    z = place("z", [P, TT, D_MODEL], F32, r_u2)
    xf = place("xf", [P, KC, SEQ], F32, r_u2 + 8192)
    hhi_last = place("hhi_last", [P, 2 * SEQ], F32R, r_u2 + 8192)
    hlo_last = place("hlo_last", [P, 2 * SEQ], F32R, r_u2 + 10240)
    g_row = place("g_row", [P, D_MODEL], F32, r_u2 + 16384)
    b_row = place("b_row", [P, D_MODEL], F32, r_u2 + 20480)
    PADW = SEQ + CONV - 1
    conv_in = place("conv_in", [P, 8, PADW], F32, r_u2)
    rv = place("rv", [P, TT, HEADS * DH], F32, r_u2)
    rg = place("rg", [P, HEADS, SEQ], F32, r_u2 + 4096)
    rot = place("rot", [P, 2 * SEQ], F32, r_u2 + 8320)
    rot_sw = place("rot_sw", [P, 2 * SEQ], F32, r_u2 + 10368)
    bc = place("bc", [P, 2, 2 * SEQ], F32, r_u2 + 12416)
    sc = place("sc", [P, 2, 384], F32, r_u2 + 16512)
    pt = place("pt", [P, 2, 384], F32, r_u2 + 19584)
    row_i = place("row_i", [HEADS, SEQ], F32, r_rows)
    row_f = place("row_f", [HEADS, SEQ], F32, r_rows + 1024)
    row_t = place("row_t", [HEADS, SEQ], F32, r_rows + 2048)
    row_m = place("row_m", [HEADS, 2 * SEQ], F32, r_rows + 3072)
    lat = place("lat", [P, QC + VC, SEQ], F32, r_y)
    lat_sq = place("lat_sq", [P, QC + VC, SEQ], F32, r_y + 5120)
    lhi = place("lhi", [P, QC + VC, SEQ], F32R, r_y + 10240)
    llo = place("llo", [P, QC + VC, SEQ], F32R, r_y + 15360)
    yhi = place("yhi", [P, 3, HEADS, SEQ], F32R, r_y)
    ylo = place("ylo", [P, 3, HEADS, SEQ], F32R, r_y + 12288)
    mhi = place("mhi", [P, KC, SEQ], F32R, r_y)
    mlo = place("mlo", [P, KC, SEQ], F32R, r_y + 12288)
    k_rope = place("k_rope", [P, SEQ], F32, r_b)
    q_nope = place("q_nope", [P, HEADS, SEQ], F32, r_b + 1024)
    q_rope = place("q_rope", [P, 2, SEQ], F32, r_b + 5120)
    k_nope = place("k_nope", [P, HEADS, SEQ], F32, r_b + 7168)
    v_mla = place("v_mla", [P, TT, HEADS * DH], F32, r_b + 11264)
    ht = place("ht", [P, 2, 2 * SEQ], F32, r_b)
    ht_sq = place("ht_sq", [P, 2 * SEQ], F32, r_b + 4096)
    ht_rs = place("ht_rs", [P, 2 * SEQ], F32, r_b + 6144)
    mo = place("mo", [P, HEADS, SEQ], F32, r_b + 8192)
    lat_rs = place("lat_rs", [P, 2 * SEQ], F32, r_b + 13312)
    ml_qk = place("ml_qk", [P, 8, SEQ], F32, r_qk)
    merged = place("merged", [P, KC, SEQ], F32, r_qk)
    ml_v = place("ml_v", [P, TT, HEADS * DH], F32, r_mv)
    gate = place("gate", [P, 4, SEQ], F32, r_mv)
    rq = place("rq", [P, HEADS, SEQ], F32, r_rq)
    rk = place("rk", [P, HEADS, SEQ], F32, r_rk)
    pos_i = place("pos_i", [P, SEQ], I32, r_y)
    pos_f = place("pos_f", [P, SEQ], F32, r_y + 1024)
    ang = place("ang", [P, SEQ], F32, r_y + 2048)
    turns = place("turns", [P, SEQ], F32, r_y + 3072)
    whole = place("whole", [P, SEQ], F32, r_y + 4096)

    ps = ctx.enter_context(nc.psum_tensor("ps", [P, 8, 512], F32))

    def C(name, n=None, off=0):
        o = CONST_AT[name] + off
        return cst[:, o:o + (n or CONST_SIZES[name])]

    def par_col(name, n):
        o = PARAM_AT[name] + n
        return par[:, o:o + 1]

    ident, ones = C("ident"), C("ones")

    square_loaded, const_loaded = sem("square_loaded"), sem("const_loaded")
    x_loaded, out_stored = sem("x_loaded"), sem("out_stored")
    w_loaded = [sem(f"w_loaded{s}") for s in range(RING)]
    w_hi, w_lo, w_used = sem("w_hi"), sem("w_lo"), sem("w_used")
    angle_step, sin_ready, sign_ready = sem("angle_step"), sem("sin_ready"), sem("sign_ready")
    x_turned, x_copied = sem("x_turned"), sem("x_copied")
    par_ready = sem("par_ready")
    silu_done, prod_done, hid_hi, hid_lo = sem("silu_done"), sem("prod_done"), sem("hid_hi"), sem("hid_lo")
    y_cleared = sem("y_cleared")
    rows_loaded = sem("rows_loaded")
    y_bank = sem("y_bank")
    ln_sum, ln_stats, ln_var, ln_std = sem("ln_sum"), sem("ln_stats"), sem("ln_var"), sem("ln_std")
    ln_rstd, ln_shift = sem("ln_rstd"), sem("ln_shift")
    ln_rows0, ln_rows1 = sem("ln_rows0"), sem("ln_rows1")
    ln_turned = sem("ln_turned")
    x_scaled, rows_scaled, xtok_ready = sem("x_scaled"), sem("rows_scaled"), sem("xtok_ready")
    x_hi, x_ready = sem("x_hi"), sem("x_ready")
    lat_copied, lat_squared, lat_summed = sem("lat_copied"), sem("lat_squared"), sem("lat_summed")
    lat_std, lat_rstd, lat_scaled = sem("lat_std"), sem("lat_rstd"), sem("lat_scaled")
    lat_hi, lat_lo = sem("lat_hi"), sem("lat_lo")
    rot_copied, rot_parts, rotated = sem("rot_copied"), sem("rot_parts"), sem("rotated")
    conv_pad, conv_copied, conv_tap, qk_silu = sem("conv_pad"), sem("conv_copied"), sem("conv_tap"), sem("qk_silu")
    q_copied, k_copied, v_copied = sem("q_copied"), sem("k_copied"), sem("v_copied")
    k_done = sem("k_done")
    mo_ready, rg_ready = sem("mo_ready"), sem("rg_ready")
    s_done, s_masked, s_max, s_negmax = sem("s_done"), sem("s_masked"), sem("s_max"), sem("s_negmax")
    s_exp, s_rsum, s_probs = sem("s_exp"), sem("s_rsum"), sem("s_probs")
    p_turned, p_copied, mla_done = sem("p_turned"), sem("p_copied"), sem("mla_done")
    f_pre, f_abs, f_exp, f_log = sem("f_pre"), sem("f_abs"), sem("f_exp"), sem("f_log")
    log_f, g_row_ready, a_row_ready, m_row_ready = sem("log_f"), sem("g_row"), sem("a_row"), sem("m_row")
    gm_row_ready, floor_ready, a_turned, a_copied = sem("gm_row"), sem("floor_row"), sem("a_turned"), sem("a_copied")
    bc_done, bc_copied, decay_arg, decay_ready = sem("bc_done"), sem("bc_copied"), sem("decay_arg"), sem("decay_ready")
    ml_scored, ml_probs, ml_summed = sem("ml_scored"), sem("ml_probs"), sem("ml_summed")
    den_step, h_ready = sem("den_step"), sem("h_ready")
    rt_scored, rt_probs, rt_summed, rt_copied = sem("rt_scored"), sem("rt_probs"), sem("rt_summed"), sem("rt_copied")
    h_means, h_centred, h_squared, h_vars = sem("h_means"), sem("h_centred"), sem("h_squared"), sem("h_vars")
    h_std, h_rstd, h_scaled, h_gated = sem("h_std"), sem("h_rstd"), sem("h_scaled"), sem("h_gated")
    y_hi, y_lo = sem("y_hi"), sem("y_lo")
    gates_ready, gate_used = sem("gates_ready"), sem("gate_used")
    branch_added, m_hi, m_lo = sem("branch_added"), sem("m_hi"), sem("m_lo")

    def unit_no(l, k, f=0):
        return l * U_LAYER + f * RING + (k + 1)

    def loaded_no(l, k, f=0):
        return (l * (U_LAYER // RING) + f + (k // RING + 1)) * 16

    free_no = unit_no

    def done_no(l, k, f=0):
        return unit_no(l, k, f) + RING

    def step_no(l, w, f):
        return l * (2 * NF) + f + (w * NF + 1)

    MIX_SIZE = ([2048, 2048, KC * 192] + [2048] * 4 + [QC * 384] * 2 + [VC * 1024] + [2048] * 2
                + [KC * 2 * HEADS] + [2048] * (MIX_FIXED - 13 + MIX_LOOP + MIX_OUT))

    def size_of(k):
        return MIX_SIZE[k - MIX_BASE] if MIX_BASE <= k < MIX_BASE + U_MIX else UNIT

    def flat(ap):
        return ap.rearrange("p a b -> p (a b)")

    def halves(ap):
        return ap.rearrange("p (a b) -> p a b", a=2)

    def twice(table):
        return table.unsqueeze(1).broadcast_to([P, 2, SEQ])

    PROJ = ["c0", "c1", "c2", "qk0", "qk1", "qk2", "qk3", "qn0", "qr", "qn1", "kn0", "kn1", "v0", "v1",
            "mv0", "mv1", "gates", "rq0", "rq1", "rk0", "rk1", "rv0", "rv1", "mo0", "mo1", "rg0", "rg1"]
    SMALL = ["rms", "S0", "S1", "T0", "T1", "pv0", "S2", "S3", "aT", "T2", "T3", "bc0", "bc1", "pv1",
             "mS0", "mS1", "mpv0", "mpv1", "bc2", "bc3", "m_mean0", "mS2", "mS3", "m_var0", "mpv2", "mpv3",
             "rS0", "rS1", "m_mean1", "rpv0", "rS2", "rS3", "m_var1", "r_mean0", "rpv1", "r_var0",
             "r_mean1", "r_var1"]
    BANK = {n: 4 + i % 4 for i, n in enumerate(PROJ)} | {n: i % 4 for i, n in enumerate(SMALL)}

    block = ctx.enter_context(nc.Block())

    @block.sync
    def _(sp):
        for s, n in ((w_used, RING), (w_lo, RING), (prod_done, 1), (hid_lo, 1),
                     (xtok_ready, 1), (gates_ready, 1), (branch_added, 1)):
            sp.sem_inc(s, n)
        sp.dma_start(cst[:, 0:2 * P], a["consts"][:, 0:2 * P]).then_inc(square_loaded, 16)
        for t in range(TT):
            sp.dma_start(xtok[:, t, :], a["x"][0, t * P:(t + 1) * P, :]).then_inc(x_loaded, 16)

        def load(l, k, src, shape, f=0):
            n = int(np.prod(shape))
            sp.wait_ge(w_lo, free_no(l, k, f))
            sp.dma_start(raw[:, k % RING, 0:n].rearrange("p (a b) -> p a b", a=shape[0]), src)\
              .then_inc(w_loaded[k % RING], 16)

        def chunks(src):
            return src.rearrange("(k p) n -> p k n", p=P)

        def load_in(l, m, lo, n):
            load(l, MIX_BASE + m, chunks(a["w_in"][l, :, lo:lo + n]), (KC, n))

        def load_rows(l, w):
            sp.wait_ge(xtok_ready, l * 6 + (2 * w + 1))
            if w == 1:
                sp.wait_ge(rt_summed, l * 2 + 2)
            for i, dst in enumerate((g_row, b_row)):
                sp.dma_start(dst[:, :], a["ln_rows"][l, w, i, :].partition_broadcast(P)).then_inc(rows_loaded, 16)

        def ffn(l, w):
            base = FFN_BASE[w]
            wg, wu, wd = (a[f"ffn{w + 1}_w_{n}"] for n in ("gate", "up", "down"))

            def cols(src, f):
                return chunks(src[l, :, bass.ds(f * FB, FB)])

            def rows(f):
                return chunks(wd[l, bass.ds(f * FB, FB), :])

            load(l, base, cols(wg, 0), (KC, FB))
            load(l, base + 1, cols(wu, 0), (KC, FB))
            with sp.Fori(0, NF - 1) as f:
                load(l, base + 2, cols(wg, f + 1), (KC, FB), f)
                load(l, base + 3, cols(wu, f + 1), (KC, FB), f)
                load(l, base + 4, rows(f), (2, D_MODEL), f)
            load_rows(l, 2 * w)
            load(l, base + 3 * NF - 1, rows(NF - 1), (2, D_MODEL))

        def mixer(l):
            load_in(l, 0, 0, 256)
            load_in(l, 1, 256, 256)
            load_in(l, 2, 512, 192)
            for i in range(4):
                load_in(l, 3 + i, C_MQ + 256 * i, 256)
            for i in range(2):
                load(l, MIX_BASE + 7 + i, chunks(a["mla_w_uq"][l, :, 384 * i:384 * i + 384]), (QC, 384))
            load(l, MIX_BASE + 9, chunks(a["mla_w_ukv"][l, :, :]), (VC, 1024))
            for i in range(2):
                load_in(l, 10 + i, C_MV + 256 * i, 256)
            load_in(l, 12, C_GATES, 2 * HEADS)
            for m, c in ((13, C_RQ), (15, C_RK), (17, C_RV), (19, C_MO), (21, C_RG)):
                for i in range(2):
                    load_in(l, m + i, c + 256 * i, 256)
            with sp.Fori(0, 3) as b:
                for h in range(2):
                    for i in range(2):
                        start = C_GL + 512 * h + 256 * i
                        load(l, MIX_BASE + 23 + 3 * h + i,
                             chunks(a["w_in"][l, :, bass.ds(b * D_MODEL + start, 256)]), (KC, 256), b * 2)
                    load(l, MIX_BASE + 25 + 3 * h, chunks(a["w_br"][l, b, :, 512 * h:512 * h + 512]),
                         (HEADS, 512), b * 2)
            load_rows(l, 1)
            for i in range(MIX_OUT):
                load(l, MIX_BASE + 41 + i, chunks(a["w_out"][l, 256 * i:256 * i + 256, :]), (2, D_MODEL))

        with sp.Fori(0, DEPTH) as l:
            ffn(l, 0)
            mixer(l)
            ffn(l, 1)
        sp.wait_ge(xtok_ready, DEPTH * 6 + 1)
        sp.dma_start(a["out"].rearrange("b (t p) d -> p (b t) d", p=P), xtok[:, :, :]).then_inc(out_stored, 16)
        sp.wait_ge(out_stored, 16)

    @block.gpsimd
    def _(pool):
        pool.wait_ge(w_loaded[RING - 1], 16)
        pool.dma_start(cst[:, 2 * P:], a["consts"][:, 2 * P:]).then_inc(const_loaded, 16)
        pool.dma_start(pos_i[:, :], a["positions"][0, :].partition_broadcast(P)).then_inc(const_loaded, 16)
        pool.dma_start(par_all[:, :, :], a["params"].rearrange("l p n -> p l n")).then_inc(const_loaded, 16)

        pool.wait_ge(const_loaded, 48)
        pool.tensor_copy(pos_f[:, :], pos_i[:, :]).then_inc(angle_step, 1)
        for n in range(4):
            quarter = 0.25 if n % 2 == 0 else 0.0
            s0 = ANGLE_STEPS * n + 1
            pool.wait_ge(angle_step, s0)
            pool.tensor_scalar(ang[:, :], pos_f[:, :], C("invf", 1, n // 2), None, ALU.mult).then_inc(angle_step, 1)
            pool.wait_ge(angle_step, s0 + 1)
            pool.tensor_scalar(turns[:, :], ang[:, :], 1 / TWO_PI, quarter, ALU.mult, ALU.add).then_inc(angle_step, 1)
            pool.wait_ge(angle_step, s0 + 2)
            pool.tensor_scalar(turns[:, :], turns[:, :], ROUND, None, ALU.add).then_inc(angle_step, 1)
            pool.wait_ge(angle_step, s0 + 3)
            pool.tensor_scalar(turns[:, :], turns[:, :], ROUND, None, ALU.subtract).then_inc(angle_step, 1)
            for i, part in enumerate((PI_A, PI_B, PI_C)):
                pool.wait_ge(angle_step, s0 + 4 + 2 * i)
                pool.tensor_scalar(whole[:, :], turns[:, :], part, None, ALU.mult).then_inc(angle_step, 1)
                pool.wait_ge(angle_step, s0 + 5 + 2 * i)
                pool.tensor_tensor(ang[:, :], ang[:, :], whole[:, :], ALU.subtract).then_inc(angle_step, 1)
            pool.wait_ge(angle_step, s0 + 10)
            pool.tensor_scalar(ang[:, :], ang[:, :], quarter * TWO_PI, None, ALU.add).then_inc(angle_step, 1)
            pool.wait_ge(angle_step, s0 + 11)
            pool.tensor_scalar(angles[:, n, :], ang[:, :], PI_MAX, -PI_MAX, ALU.min, ALU.max).then_inc(angle_step, 1)
        pool.wait_ge(angle_step, 4 * ANGLE_STEPS + 1)
        for n in (1, 3):
            pool.tensor_scalar(angles[:, n, :], angles[:, n, :], C("sign", 1, n // 2), None,
                               ALU.mult).then_inc(sign_ready, 1)

        with pool.Fori(0, DEPTH) as l:
            for w in range(3):
                pool.wait_ge(rows_loaded, l * 96 + 32 * (w + 1))
                for t in range(TT):
                    pool.wait_ge(ln_rows1 if t else ln_rows0, l * 6 + (2 * w + 2))
                    pool.tensor_tensor(xtok[:, t, :], z[:, t, :], g_row[:, :], ALU.mult).then_inc(rows_scaled, 1)
                for t in range(TT):
                    pool.wait_ge(rows_scaled, l * 6 + (2 * w + t + 1))
                    pool.tensor_tensor(xtok[:, t, :], xtok[:, t, :], b_row[:, :], ALU.add).then_inc(xtok_ready, 1)

    @block.scalar
    def _(act):
        def hi(l, k, f=0):
            n = size_of(k)
            act.wait_ge(w_loaded[k % RING], loaded_no(l, k, f))
            act.wait_ge(w_used, free_no(l, k, f))
            act.activation(whi[:, k % RING, 0:n], raw[:, k % RING, 0:n], ACT.Copy).then_inc(w_hi, 1)

        def ffn(l, w):
            base = FFN_BASE[w]
            if w == 0:
                hi(l, base)
                hi(l, base + 1)
            act.wait_ge(xtok_ready, l * 6 + (4 * w + 1))

            def silu_of(j, k, f):
                act.wait_ge(w_used, done_no(l, k, f))
                act.wait_ge(prod_done, step_no(l, w, j))
                act.activation(silu[:, :], ps[:, 4, :], ACT.Silu).then_inc(silu_done, 1)

            hi(l, base + 2)
            silu_of(0, base, 0)
            hi(l, base + 3)
            hi(l, base + 4)
            with act.Fori(0, NF - 2) as f:
                hi(l, base + 5, f)
                silu_of(f + 1, base + 2, f)
                hi(l, base + 6, f)
                hi(l, base + 7, f)
            silu_of(NF - 1, base + 2, NF - 2)
            hi(l, base + 3 * NF - 1)

        def layer_norm(l, w, early):
            for k in early[:2]:
                hi(l, k)
            act.wait_ge(par_ready, l + 1)
            act.activation(warm[:, :], C("eps", 1), ACT.Sqrt)

            def root(t):
                act.wait_ge(ln_var, l * 6 + (2 * w + t + 1))
                act.activation(std[:, t:t + 1], mv[:, t, 1:2], ACT.Sqrt,
                               bias=C("eps", 1, 0 if w == 1 else 1)).then_inc(ln_std, 1)

            def half_rows(c):
                part = slice(512 * c, 512 * c + 512)
                act.activation(z[:, 0, part], z[:, 0, part], ACT.Identity, bias=shift[:, :],
                               scale=rstd[:, 0:1]).then_inc(ln_rows0, 1)

            root(0)
            act.wait_ge(ln_shift, l * 3 + (w + 1))
            half_rows(0)
            root(1)
            half_rows(1)
            for pair in range(4):
                act.wait_ge(ln_turned, l * 12 + (4 * w + pair + 1))
                for k in (2 * pair, 2 * pair + 1):
                    last = act.activation(xf[:, k, :], ps[:, 4 + pair, (k % 2) * SEQ:(k % 2 + 1) * SEQ], ACT.Identity,
                                          bias=par_col("ln_b", 8 * w + k), scale=par_col("ln_g", 8 * w + k))
                last.then_inc(x_scaled, 1)
            for k in early[2:]:
                hi(l, k)

        def mixer(l):
            m0 = MIX_BASE

            def copy(dst, job, lo=0, n=512, func=ACT.Copy, src=slice(0, P)):
                return act.activation(dst, ps[src, BANK[job], lo:lo + n], func)

            def swap(job, half):
                copy(rot[:, :], job)
                for p0 in range(0, P, half):
                    p1 = p0 ^ half
                    last = copy(rot_sw[p0:p0 + half, :], job, src=slice(p1, p1 + half))
                return last

            def exps(h):
                act.wait_ge(s_negmax, l * 4 + (h + 1))
                for q, (c0, c1) in enumerate(((0, P), (P, 3 * P))):
                    last = act.activation(sc[:, h % 2, c0:c1], sc[:, h % 2, c0:c1], ACT.Exp,
                                          bias=mx[:, h, q:q + 1], accum_out=rowsum[:, h, q:q + 1])
                last.then_inc(s_exp, 1)

            def pt_copy(h):
                act.wait_ge(p_turned, l * 4 + (h + 1))
                copy(pt[:, h % 2, :], f"T{h}", 0, 384).then_inc(p_copied, 1)

            def bc_copy(h):
                act.wait_ge(bc_done, l * 4 + (h + 1))
                copy(bc[:, h % 2, :], f"bc{h}").then_inc(bc_copied, 1)

            def decay(h):
                act.wait_ge(decay_arg, l * 4 + (h + 1))
                act.activation(sc[:, h % 2, :], sc[:, h % 2, :], ACT.Exp, scale=-1.0).then_inc(decay_ready, 1)

            def norm_std(n):
                act.wait_ge(h_vars, l * 4 + (n + 1))
                if n:
                    act.wait_ge(h_scaled, l * 4 + n)
                act.activation(ht_rs[:, :], ps[:, BANK[f"{'mr'[n // 2]}_var{n % 2}"], :], ACT.Sqrt,
                               scale=1.0 / DH, bias=C("eps", 1)).then_inc(h_std, 1)

            hi(l, m0 + 3)
            act.wait_ge(sign_ready, 2)
            act.activation(tables[:, :, :], angles[:, :, :], ACT.Sin).then_inc(sin_ready, 1)
            act.wait_ge(w_used, done_no(l, m0))
            copy(flat(lat[:, 0:2, :]), "c0").then_inc(lat_copied, 1)
            hi(l, m0 + 4)
            act.wait_ge(w_used, done_no(l, m0 + 1))
            copy(flat(lat[:, 2:4, :]), "c1").then_inc(lat_copied, 1)
            hi(l, m0 + 5)
            act.wait_ge(w_used, done_no(l, m0 + 2))
            copy(lat[:, 4, :], "c2", 0, SEQ).then_inc(lat_copied, 1)
            for p0 in (0, ROPE):
                copy(rot[p0:p0 + ROPE, 0:SEQ], "c2", SEQ, SEQ, src=slice(0, ROPE))
            for i in range(4):
                p0, p1 = 32 * i, 32 * (1 - i % 2)
                last = copy(rot_sw[p0:p0 + 32, 0:SEQ], "c2", SEQ, SEQ, src=slice(p1, p1 + 32))
            last.then_inc(rot_copied, 1)
            hi(l, m0 + 6)
            act.wait_ge(lat_summed, l + 1)
            act.activation(lat_rs[:, 0:SEQ], ps[:, BANK["rms"], 0:SEQ], ACT.Sqrt, scale=1.0 / Q_LORA, bias=C("eps", 1))
            act.activation(lat_rs[:, SEQ:], ps[:, BANK["rms"], SEQ:], ACT.Sqrt, scale=1.0 / KV_LORA,
                           bias=C("eps", 1)).then_inc(lat_std, 1)
            act.wait_ge(xtok_ready, l * 6 + 3)
            for i in range(4):
                act.wait_ge(w_used, done_no(l, m0 + 3 + i))
                act.activation(conv_in[:, 2 * i:2 * i + 2, CONV - 1:PADW], halves(ps[:, BANK[f"qk{i}"], :]),
                               ACT.Copy).then_inc(conv_copied, 1)
                hi(l, m0 + 7 + i)
            act.wait_ge(w_used, done_no(l, m0 + 7))
            copy(flat(q_nope[:, 0:2, :]), "qn0").then_inc(q_copied, 1)
            act.wait_ge(w_used, done_no(l, m0 + 8))
            act.wait_ge(rotated, l * 6 + 1)
            swap("qr", 32).then_inc(rot_copied, 1)
            copy(flat(q_nope[:, 2:4, :]), "qn1").then_inc(q_copied, 1)
            hi(l, m0 + 11)
            act.wait_ge(conv_tap, l * 32 + 16)
            act.activation(ml_qk[:, 0:4, :], ml_qk[:, 0:4, :], ACT.Silu).then_inc(qk_silu, 1)
            act.wait_ge(k_done, l + 1)
            copy(flat(k_nope[:, 0:2, :]), "kn0").then_inc(k_copied, 1)
            copy(flat(k_nope[:, 2:4, :]), "kn1").then_inc(k_copied, 1)
            hi(l, m0 + 12)
            hi(l, m0 + 13)
            hi(l, m0 + 14)
            exps(0)
            exps(1)
            hi(l, m0 + 15)
            act.wait_ge(f_abs, l + 1)
            act.activation(row_t[:, :], row_t[:, :], ACT.Exp, scale=-1.0).then_inc(f_exp, 1)
            act.wait_ge(f_exp, l + 1)
            act.activation(row_t[:, :], row_t[:, :], ACT.Ln, bias=C("one")[0:HEADS, :]).then_inc(f_log, 1)
            act.wait_ge(conv_tap, l * 32 + 32)
            act.activation(ml_qk[:, 4:8, :], ml_qk[:, 4:8, :], ACT.Silu).then_inc(qk_silu, 1)
            pt_copy(0)
            pt_copy(1)
            hi(l, m0 + 16)
            act.wait_ge(gm_row_ready, l + 1)
            act.activation(row_m[:, SEQ:], row_t[:, :], ACT.Exp, scale=-1.0).then_inc(floor_ready, 1)
            act.wait_ge(w_used, done_no(l, m0 + 13))
            act.wait_ge(rotated, l * 6 + 2)
            swap("rq0", 64).then_inc(rot_copied, 1)
            exps(2)
            exps(3)
            hi(l, m0 + 17)
            act.wait_ge(w_used, done_no(l, m0 + 14))
            act.wait_ge(rotated, l * 6 + 3)
            swap("rq1", 64).then_inc(rot_copied, 1)
            act.wait_ge(mla_done, l * 2 + 1)
            pt_copy(2)
            pt_copy(3)
            hi(l, m0 + 18)
            bc_copy(0)
            bc_copy(1)
            act.wait_ge(w_used, done_no(l, m0 + 15))
            act.wait_ge(rotated, l * 6 + 4)
            swap("rk0", 64).then_inc(rot_copied, 1)
            decay(0)
            decay(1)
            hi(l, m0 + 19)
            act.wait_ge(w_used, done_no(l, m0 + 16))
            act.wait_ge(rotated, l * 6 + 5)
            swap("rk1", 64).then_inc(rot_copied, 1)
            hi(l, m0 + 20)
            act.wait_ge(h_ready, l * 4 + 2)
            bc_copy(2)
            bc_copy(3)
            hi(l, m0 + 21)
            decay(2)
            decay(3)
            norm_std(0)
            hi(l, m0 + 22)
            act.wait_ge(w_used, done_no(l, m0 + 19))
            copy(flat(mo[:, 0:2, :]), "mo0", func=ACT.Sigmoid).then_inc(mo_ready, 1)
            hi(l, m0 + 23)
            act.wait_ge(w_used, done_no(l, m0 + 20))
            copy(flat(mo[:, 2:4, :]), "mo1", func=ACT.Sigmoid).then_inc(mo_ready, 1)
            norm_std(1)
            hi(l, m0 + 24)
            act.wait_ge(w_used, done_no(l, m0 + 21))
            copy(flat(rg[:, 0:2, :]), "rg0", func=ACT.Silu).then_inc(rg_ready, 1)
            hi(l, m0 + 25)
            act.wait_ge(w_used, done_no(l, m0 + 22))
            copy(flat(rg[:, 2:4, :]), "rg1", func=ACT.Silu).then_inc(rg_ready, 1)

            for b in range(3):
                turn = l * 3 + b
                for h in range(2):
                    for i in range(3):
                        hi(l, m0 + 26 + 6 * b + 3 * h + i)
                        if i == 2:
                            continue
                        act.wait_ge(w_used, done_no(l, m0 + 23 + 6 * b + 3 * h + i))
                        act.wait_ge(branch_added, turn * 4 + (2 + i if h else 1))
                        if b == h == 0:
                            act.wait_ge(ml_summed, l * 4 + 4)
                        for c in range(2):
                            last = act.activation(gate[:, 2 * i + c, :], ps[:, 4 + i, c * SEQ:(c + 1) * SEQ],
                                                  ACT.Sigmoid, bias=par_col("gate_b", KC * b + 4 * h + 2 * i + c))
                        last.then_inc(gates_ready, 1)
                        if b == h == 0:
                            norm_std(2 + i)
            hi(l, m0 + 44)

        act.wait_ge(x_turned, 1)
        for j in range(4):
            act.activation(flat(xf[:, 2 * j:2 * j + 2, :]), ps[:, 4 + j, :], ACT.Copy).then_inc(x_copied, 1)

        with act.Fori(0, DEPTH) as l:
            ffn(l, 0)
            layer_norm(l, 0, [MIX_BASE, MIX_BASE + 1, MIX_BASE + 2])
            mixer(l)
            layer_norm(l, 1, [FFN_BASE[1], FFN_BASE[1] + 1])
            ffn(l, 1)
            layer_norm(l, 2, [])

    @block.vector
    def _(dve):
        def lo(l, k, f=0):
            n = size_of(k)
            dve.wait_ge(w_hi, unit_no(l, k, f))
            dve.tensor_tensor(wlo[:, k % RING, 0:n], raw[:, k % RING, 0:n],
                              whi[:, k % RING, 0:n].bitcast(F32), ALU.subtract).then_inc(w_lo, 1)

        def ffn(l, w):
            base = FFN_BASE[w]
            if w == 0:
                lo(l, base)
            dve.memset(ps[:, 0:4, :], 0.0).then_inc(y_cleared, 1)
            if w == 0:
                lo(l, base + 1)
            dve.wait_ge(xtok_ready, l * 6 + (4 * w + 1))

            def product(j, k, f):
                dve.wait_ge(silu_done, step_no(l, w, j))
                dve.wait_ge(w_used, done_no(l, k, f))
                dve.wait_ge(hid_lo, step_no(l, w, j))
                dve.tensor_tensor(hid[:, :], silu[:, :], ps[:, 5, :], ALU.mult).then_inc(prod_done, 1)

            def split(j, f, dst_hi=hhi, dst_lo=hlo):
                dve.wait_ge(prod_done, step_no(l, w, j) + 1)
                if f is not None:
                    dve.wait_ge(w_used, done_no(l, base + 4, f))
                dve.tensor_copy(dst_hi[:, :], hid[:, :]).then_inc(hid_hi, 1)
                dve.wait_ge(hid_hi, step_no(l, w, j))
                dve.tensor_tensor(dst_lo[:, :], hid[:, :], dst_hi[:, :].bitcast(F32),
                                  ALU.subtract).then_inc(hid_lo, 1)

            lo(l, base + 2)
            product(0, base + 1, 0)
            lo(l, base + 3)
            split(0, None)
            lo(l, base + 4)
            with dve.Fori(0, NF - 2) as f:
                lo(l, base + 5, f)
                product(f + 1, base + 3, f)
                lo(l, base + 6, f)
                split(f + 1, f)
                lo(l, base + 7, f)
            product(NF - 1, base + 3, NF - 2)
            split(NF - 1, None, hhi_last, hlo_last)
            lo(l, base + 3 * NF - 1)

        def split_x(pair, stage):
            part = slice(2 * pair, 2 * pair + 2)
            dve.tensor_copy(xhi[:, part, :], xf[:, part, :]).then_inc(x_hi, 1)
            dve.wait_ge(x_hi, stage * 4 + (pair + 1))
            dve.tensor_tensor(xlo[:, part, :], xf[:, part, :], xhi[:, part, :].bitcast(F32),
                              ALU.subtract).then_inc(x_ready, 1)

        def layer_norm(l, w, early):
            turn = l * 3 + w
            coef = ALPHA if w == 1 else 2 * ALPHA
            for k in early[:1]:
                lo(l, k)
            dve.wait_ge(xtok_ready, turn * 2 + 1)
            dve.wait_ge(x_loaded, 16 * TT)

            def add_x(b):
                t, part = b // 2, slice(512 * (b % 2), 512 * (b % 2) + 512)
                if b < 3:
                    dve.wait_ge(y_bank, turn * 3 + (b + 1))
                else:
                    dve.wait_ge(w_used, done_no(l, MIX_BASE + U_MIX - 1 if w == 1 else FFN_BASE[w // 2] + U_FFN - 1))
                dve.scalar_tensor_tensor(out=z[:, t, part], in0=xtok[:, t, part], scalar=coef, in1=ps[:, b, :],
                                         op0=ALU.mult, op1=ALU.add).then_inc(ln_sum, 1)

            def measure(b):
                dve.wait_ge(ln_sum, turn * 4 + (b + 1))
                dve.bn_stats(stats[:, b // 2, b % 2, :], z[:, b // 2, 512 * (b % 2):512 * (b % 2) + 512])\
                   .then_inc(ln_stats, 1)

            def aggregate(t):
                dve.bn_aggr(mv[:, t, :], flat(stats[:, t, :, :])).then_inc(ln_var, 1)

            def invert(t):
                dve.wait_ge(ln_std, turn * 2 + (t + 1))
                dve.reciprocal(rstd[:, t:t + 1], std[:, t:t + 1]).then_inc(ln_rstd, 1)
                dve.wait_ge(ln_rstd, turn * 2 + (t + 1))

            add_x(0)
            measure(0)
            add_x(1)
            measure(1)
            dve.wait_ge(ln_stats, turn * 4 + 2)
            add_x(2)
            aggregate(0)
            measure(2)
            add_x(3)
            invert(0)
            dve.scalar_tensor_tensor(out=shift[:, :], in0=mv[:, 0, 0:1], scalar=-1.0, in1=rstd[:, 0:1],
                                     op0=ALU.mult, op1=ALU.mult).then_inc(ln_shift, 1)
            measure(3)
            dve.wait_ge(ln_stats, turn * 4 + 4)
            dve.memset(pause[:, :], 0.0)
            aggregate(1)
            invert(1)
            for c in range(2):
                part = slice(512 * c, 512 * c + 512)
                dve.tensor_scalar(z[:, 1, part], z[:, 1, part], mv[:, 1, 0:1], rstd[:, 1:2],
                                  ALU.subtract, ALU.mult).then_inc(ln_rows1, 1)
            for k in early[1:2]:
                lo(l, k)
            for pair in range(4):
                dve.wait_ge(x_scaled, turn * 4 + (pair + 1))
                split_x(pair, turn + 1)
            for k in early[2:]:
                lo(l, k)

        def mixer(l):
            m0 = MIX_BASE

            def stt(out, in0, scalar, op0, in1, op1):
                return dve.scalar_tensor_tensor(out=out, in0=in0, scalar=scalar, in1=in1, op0=op0, op1=op1)

            def rotate(r, dst, cos, sin, n=2):
                def wide(x):
                    return halves(x[:, :]) if n == 2 else x[:, 0:SEQ]
                factors = [twice(t) if n == 2 else t for t in (cos, sin)]
                dve.wait_ge(sin_ready, l + 1)
                dve.wait_ge(rot_copied, l * 6 + (r + 1))
                dve.tensor_tensor(wide(rot), wide(rot), factors[0], ALU.mult)
                dve.tensor_tensor(wide(rot_sw), wide(rot_sw), factors[1], ALU.mult).then_inc(rot_parts, 1)
                dve.wait_ge(rot_parts, l * 6 + (r + 1))
                dve.tensor_tensor(dst, wide(rot), wide(rot_sw), ALU.add).then_inc(rotated, 1)

            def conv(i):
                dve.wait_ge(conv_copied, l * 4 + (i + 1))
                dve.wait_ge(conv_pad, l + 1)
                for n, tap in enumerate(range(CONV - 1, -1, -1)):
                    for c, j in enumerate((2 * i, 2 * i + 1)):
                        col = par_col("conv_w", 8 * tap + j)
                        shifted = conv_in[:, j, tap:tap + SEQ]
                        if n == 0:
                            dve.tensor_scalar(ml_qk[:, j, :], shifted, col, par_col("conv_b", j),
                                              ALU.mult, ALU.add).then_inc(conv_tap, 1)
                        else:
                            dve.wait_ge(conv_tap, l * 32 + (8 * i + 2 * (n - 1) + c + 1))
                            stt(ml_qk[:, j, :], shifted, col, ALU.mult, ml_qk[:, j, :], ALU.add).then_inc(conv_tap, 1)

            def scores(h):
                dve.wait_ge(s_done, l * 4 + (h + 1))
                if h >= 2:
                    dve.wait_ge(p_turned, l * 4 + (h - 1))
                stt(sc[:, h % 2, :], ps[:, BANK[f"S{h}"], 0:384], MLA_SCALE, ALU.mult, C("mask"),
                    ALU.add).then_inc(s_masked, 1)
                dve.wait_ge(s_masked, l * 4 + (h + 1))
                for q, (c0, c1) in enumerate(((0, P), (P, 3 * P))):
                    last = dve.tensor_reduce(mx[:, h, q:q + 1], sc[:, h % 2, c0:c1], AX.X, ALU.max)
                last.then_inc(s_max, 1)
                dve.wait_ge(s_max, l * 4 + (h + 1))
                dve.tensor_scalar(mx[:, h, :], mx[:, h, :], -1.0, None, ALU.mult).then_inc(s_negmax, 1)

            def probs(h):
                dve.wait_ge(s_exp, l * 4 + (h + 1))
                dve.reciprocal(rinv[:, h, :], rowsum[:, h, :]).then_inc(s_rsum, 1)
                dve.wait_ge(s_rsum, l * 4 + (h + 1))
                for q, (c0, c1) in enumerate(((0, P), (P, 3 * P))):
                    last = dve.tensor_scalar(sc[:, h % 2, c0:c1], sc[:, h % 2, c0:c1], rinv[:, h, q:q + 1],
                                             None, ALU.mult)
                last.then_inc(s_probs, 1)

            def split_y(n, src):
                hi_p, lo_p = (flat(t[:, n // 2, 2 * (n % 2):2 * (n % 2) + 2, :]) for t in (yhi, ylo))
                dve.tensor_copy(hi_p, src).then_inc(y_hi, 1)
                dve.wait_ge(y_hi, l * 6 + (n + 1))
                dve.tensor_tensor(lo_p, src, hi_p.bitcast(F32), ALU.subtract).then_inc(y_lo, 1)

            def y_mla(p):
                dve.wait_ge(mla_done, l * 2 + (p + 1))
                split_y(p, ps[:, BANK[f"pv{p}"], :])

            def args(h):
                dve.wait_ge(bc_copied, l * 4 + (h + 1))
                dve.wait_ge(a_copied, l + 1)
                if h < 2:
                    dve.wait_ge(p_turned, l * 4 + (h + 3))
                else:
                    dve.wait_ge(ml_summed, l * 4 + (h - 1))
                stt(sc[:, h % 2, 0:SEQ], bc[:, h % 2, 0:SEQ], a_col[:, 0, h:h + 1], ALU.subtract,
                    C("pmask", SEQ), ALU.add)
                stt(sc[:, h % 2, SEQ:384], bc[:, h % 2, P:SEQ], a_col[:, 1, h:h + 1], ALU.subtract,
                    C("pmask", P, SEQ), ALU.add).then_inc(decay_arg, 1)

            def weigh(h):
                dve.wait_ge(ml_scored, l * 4 + (h + 1))
                dve.wait_ge(decay_ready, l * 4 + (h + 1))
                stt(sc[:, h % 2, :], ps[:, BANK[f"mS{h}"], 0:384], HEAD_SCALE, ALU.mult, sc[:, h % 2, :],
                    ALU.mult).then_inc(ml_probs, 1)

            def ml_out(h):
                bank = ps[:, BANK[f"mpv{h}"], :]
                floor = bc[:, h % 2, SEQ:]
                dve.wait_ge(ml_summed, l * 4 + (h + 1))
                stt(floor, bank[:, SEQ:], -1.0, ALU.mult, floor, ALU.max).then_inc(den_step, 1)
                dve.wait_ge(den_step, l * 12 + (3 * h + 1))
                dve.tensor_tensor(floor, bank[:, SEQ:], floor, ALU.max).then_inc(den_step, 1)
                dve.wait_ge(den_step, l * 12 + (3 * h + 2))
                dve.reciprocal(floor, floor).then_inc(den_step, 1)
                dve.wait_ge(den_step, l * 12 + (3 * h + 3))
                dve.tensor_tensor(ht[:, h // 2, (h % 2) * SEQ:(h % 2 + 1) * SEQ], bank[:, 0:SEQ], floor,
                                  ALU.mult).then_inc(h_ready, 1)

            def center(n):
                p = n % 2
                dve.wait_ge(h_means, l * 4 + (n + 1))
                stt(ht[:, p, :], ps[:, BANK[f"{'mr'[n // 2]}_mean{p}"], :], -1.0 / DH, ALU.mult, ht[:, p, :],
                    ALU.add).then_inc(h_centred, 1)
                dve.wait_ge(h_centred, l * 4 + (n + 1))
                if n:
                    dve.wait_ge(h_vars, l * 4 + n)
                dve.tensor_tensor(ht_sq[:, :], ht[:, p, :], ht[:, p, :], ALU.mult).then_inc(h_squared, 1)

            def normalise(n):
                p = n % 2
                dve.wait_ge(h_std, l * 4 + (n + 1))
                dve.reciprocal(ht_rs[:, :], ht_rs[:, :]).then_inc(h_rstd, 1)
                dve.wait_ge(h_rstd, l * 4 + (n + 1))
                for i in range(2):
                    part = slice(i * SEQ, (i + 1) * SEQ)
                    last = stt(ht[:, p, part], ht[:, p, part], par_col("ml_g" if n < 2 else "rt_g", 2 * p + i),
                               ALU.mult, ht_rs[:, part], ALU.mult)
                last.then_inc(h_scaled, 1)
                dve.wait_ge(mo_ready if n < 2 else rg_ready, l * 2 + (p + 1))
                dve.wait_ge(h_scaled, l * 4 + (n + 1))
                dve.tensor_tensor(ht[:, p, :], ht[:, p, :], flat((mo if n < 2 else rg)[:, 2 * p:2 * p + 2, :]),
                                  ALU.mult).then_inc(h_gated, 1)
                dve.wait_ge(h_gated, l * 4 + (n + 1))
                split_y(n + 2, ht[:, p, :])

            def ret_probs(h):
                dve.wait_ge(rt_scored, l * 4 + (h + 1))
                if h >= 2:
                    dve.wait_ge(rt_summed, l * 2 + 1)
                stt(pt[:, h % 2, :], ps[:, BANK[f"rS{h}"], 0:384], HEAD_SCALE, ALU.mult,
                    C("decay", 384, 384 * h), ALU.mult).then_inc(rt_probs, 1)

            def ret_out(p):
                dve.wait_ge(rt_summed, l * 2 + (p + 1))
                dve.wait_ge(y_lo, l * 6 + (p + 3))
                dve.tensor_copy(ht[:, p, :], ps[:, BANK[f"rpv{p}"], :]).then_inc(rt_copied, 1)

            dve.wait_ge(xtok_ready, l * 6 + 3)
            dve.memset(conv_in[:, :, 0:CONV - 1], 0.0).then_inc(conv_pad, 1)
            lo(l, m0 + 3)
            for i in range(3):
                part = slice(2 * i, min(2 * i + 2, QC + VC))
                dve.wait_ge(lat_copied, l * 3 + (i + 1))
                dve.tensor_tensor(lat_sq[:, part, :], lat[:, part, :], lat[:, part, :],
                                  ALU.mult).then_inc(lat_squared, 1)
                if i < 2:
                    lo(l, m0 + 4 + i)
            rotate(0, k_rope[:, :], cos_m, sin_m, 1)
            lo(l, m0 + 6)
            dve.wait_ge(lat_std, l + 1)
            dve.reciprocal(lat_rs[:, :], lat_rs[:, :]).then_inc(lat_rstd, 1)
            dve.wait_ge(lat_rstd, l + 1)
            for c in range(QC + VC):
                g = par_col("q_g", c) if c < QC else par_col("kv_g", c - QC)
                last = stt(lat[:, c, :], lat[:, c, :], g, ALU.mult,
                           lat_rs[:, 0:SEQ] if c < QC else lat_rs[:, SEQ:], ALU.mult)
            last.then_inc(lat_scaled, 1)
            dve.wait_ge(lat_scaled, l + 1)
            dve.tensor_copy(lhi[:, :, :], lat[:, :, :]).then_inc(lat_hi, 1)
            dve.wait_ge(lat_hi, l + 1)
            dve.tensor_tensor(llo[:, :, :], lat[:, :, :], lhi[:, :, :].bitcast(F32), ALU.subtract).then_inc(lat_lo, 1)
            conv(0)
            lo(l, m0 + 7)
            conv(1)
            lo(l, m0 + 8)
            lo(l, m0 + 9)
            conv(2)
            lo(l, m0 + 10)
            lo(l, m0 + 11)
            rotate(1, q_rope[:, :, :], cos_m, sin_m)
            lo(l, m0 + 12)
            dve.wait_ge(w_used, done_no(l, m0 + 9))
            for t in range(TT):
                dve.tensor_copy(v_mla[:, t, :], ps[:, BANK[f"v{t}"], :]).then_inc(v_copied, 1)
            lo(l, m0 + 13)
            dve.wait_ge(w_used, done_no(l, m0 + 11))
            for t in range(TT):
                dve.tensor_copy(ml_v[:, t, :], ps[:, BANK[f"mv{t}"], :]).then_inc(v_copied, 1)
            lo(l, m0 + 14)
            scores(0)
            scores(1)
            gbank = ps[0:HEADS, BANK["gates"], :]
            dve.wait_ge(w_used, done_no(l, m0 + 12))
            dve.tensor_scalar(row_i[:, :], gbank[:, 0:SEQ], par_col("i_b", 0)[0:HEADS, :], None, ALU.add)
            dve.tensor_scalar(row_f[:, :], gbank[:, SEQ:], par_col("f_b", 0)[0:HEADS, :], None,
                              ALU.add).then_inc(f_pre, 1)
            dve.wait_ge(f_pre, l + 1)
            stt(row_t[:, :], row_f[:, :], -1.0, ALU.mult, row_f[:, :], ALU.max).then_inc(f_abs, 1)
            probs(0)
            probs(1)
            conv(3)
            lo(l, m0 + 15)
            dve.wait_ge(f_log, l + 1)
            dve.memset(row_m[:, SEQ:], 0.0)
            stt(row_f[:, :], row_f[:, :], 0.0, ALU.min, row_t[:, :], ALU.subtract).then_inc(log_f, 1)
            dve.wait_ge(log_f, l + 1)
            dve.tensor_tensor_scan(row_t[:, :], row_f[:, :], row_m[:, SEQ:], 0.0, ALU.add,
                                   ALU.add).then_inc(g_row_ready, 1)
            dve.wait_ge(g_row_ready, l + 1)
            dve.tensor_tensor(row_i[:, :], row_i[:, :], row_t[:, :], ALU.subtract).then_inc(a_row_ready, 1)
            dve.wait_ge(a_row_ready, l + 1)
            dve.tensor_tensor_scan(row_m[:, 0:SEQ], row_i[:, :], row_i[:, :], 0.0, ALU.max,
                                   ALU.max).then_inc(m_row_ready, 1)
            dve.wait_ge(m_row_ready, l + 1)
            dve.tensor_tensor(row_t[:, :], row_t[:, :], row_m[:, 0:SEQ], ALU.add).then_inc(gm_row_ready, 1)
            lo(l, m0 + 16)
            y_mla(0)
            scores(2)
            scores(3)
            dve.wait_ge(a_turned, l + 1)
            dve.tensor_copy(flat(a_col[:, :, :]), ps[:, BANK["aT"], 0:TT * HEADS]).then_inc(a_copied, 1)
            probs(2)
            probs(3)
            rotate(2, rq[:, 0:2, :], cos_r, sin_r)
            lo(l, m0 + 17)
            rotate(3, rq[:, 2:4, :], cos_r, sin_r)
            lo(l, m0 + 18)
            args(0)
            args(1)
            y_mla(1)
            weigh(0)
            weigh(1)
            rotate(4, rk[:, 0:2, :], cos_r, sin_r)
            lo(l, m0 + 19)
            ml_out(0)
            ml_out(1)
            rotate(5, rk[:, 2:4, :], cos_r, sin_r)
            lo(l, m0 + 20)
            center(0)
            args(2)
            args(3)
            weigh(2)
            weigh(3)
            dve.wait_ge(w_used, done_no(l, m0 + 18))
            for t in range(TT):
                dve.tensor_copy(rv[:, t, :], ps[:, BANK[f"rv{t}"], :]).then_inc(v_copied, 1)
            lo(l, m0 + 21)
            ml_out(2)
            ml_out(3)
            ret_probs(0)
            ret_probs(1)
            lo(l, m0 + 22)
            normalise(0)
            center(1)
            ret_out(0)
            ret_probs(2)
            ret_probs(3)
            lo(l, m0 + 23)
            center(2)
            lo(l, m0 + 24)
            normalise(1)
            ret_out(1)
            lo(l, m0 + 25)

            for b in range(3):
                turn = l * 3 + b
                for h in range(2):
                    lo(l, m0 + 26 + 6 * b + 3 * h)
                    if b == h == 0:
                        center(3)
                        normalise(2)
                    lo(l, m0 + 27 + 6 * b + 3 * h)
                    if b == h == 0:
                        normalise(3)
                    dve.wait_ge(w_used, done_no(l, m0 + 25 + 6 * b + 3 * h))
                    dve.wait_ge(gates_ready, turn * 4 + (2 * h + 3))
                    for c in range(2):
                        part = gate[:, 2 * c:2 * c + 2, :]
                        dst = merged[:, 4 * h + 2 * c:4 * h + 2 * c + 2, :]
                        if b == 0:
                            dve.tensor_tensor(dst, halves(ps[:, 6 + c, :]), part, ALU.mult).then_inc(branch_added, 1)
                        else:
                            dve.tensor_tensor(part, halves(ps[:, 6 + c, :]), part, ALU.mult).then_inc(gate_used, 1)
                    for c in range(2):
                        if b:
                            dst = merged[:, 4 * h + 2 * c:4 * h + 2 * c + 2, :]
                            dve.wait_ge(gate_used, l * 8 + (4 * b + 2 * h + c - 3))
                            dve.wait_ge(branch_added, turn * 4 + (2 * h + c - 2))
                            dve.tensor_tensor(dst, dst, gate[:, 2 * c:2 * c + 2, :], ALU.add).then_inc(branch_added, 1)
                    if b == 2:
                        for i in (2 * h, 2 * h + 1):
                            part = slice(2 * i, 2 * i + 2)
                            dve.wait_ge(branch_added, turn * 4 + (i + 2))
                            dve.tensor_copy(mhi[:, part, :], merged[:, part, :]).then_inc(m_hi, 1)
                            dve.wait_ge(m_hi, l * 4 + (i + 1))
                            dve.tensor_tensor(mlo[:, part, :], merged[:, part, :], mhi[:, part, :].bitcast(F32),
                                              ALU.subtract).then_inc(m_lo, 1)
                    lo(l, m0 + 28 + 6 * b + 3 * h)
            lo(l, m0 + 44)

        for pair in range(4):
            dve.wait_ge(x_copied, pair + 1)
            split_x(pair, 0)

        with dve.Fori(0, DEPTH) as l:
            ffn(l, 0)
            dve.wait_ge(const_loaded, 48)
            dve.tensor_copy(par[:, :], par_all[:, bass.ds(l, 1), :].rearrange("p a b -> p (a b)")).then_inc(par_ready, 1)
            layer_norm(l, 0, [MIX_BASE, MIX_BASE + 1, MIX_BASE + 2])
            mixer(l)
            layer_norm(l, 1, [FFN_BASE[1], FFN_BASE[1] + 1])
            ffn(l, 1)
            layer_norm(l, 2, [])

    @block.tensor
    def _(pe):
        def tile3(out, w_hi_ap, w_lo_ap, x_hi_ap, x_lo_ap, start, stop):
            pe.matmul(out, w_hi_ap, x_hi_ap, start=start, stop=False)
            pe.matmul(out, w_hi_ap, x_lo_ap, start=False, stop=False)
            return pe.matmul(out, w_lo_ap, x_hi_ap, start=False, stop=stop)

        def slot(k, width):
            n = size_of(k)
            return tuple(t[:, k % RING, 0:n].rearrange("p (k n) -> p k n", n=width) for t in (whi, wlo))

        def features(out, k, width, cols, xh, xl, n_k, stage=None):
            wh, wl = slot(k, width)
            for kk in range(n_k):
                if stage is not None and kk % 2 == 0:
                    pe.wait_ge(x_ready, stage * 4 + (kk // 2 + 1))
                last = tile3(out, wh[:, kk, cols], wl[:, kk, cols], xh(kk), xl(kk), kk == 0, kk == n_k - 1)
            return last

        def x_h(kk):
            return xhi[:, kk, :]

        def x_l(kk):
            return xlo[:, kk, :]

        def two_chunks(bank, k, width=256, n_k=KC, xh=x_h, xl=x_l, stage=None):
            for c in range(2):
                last = features(ps[:, bank, c * SEQ:(c + 1) * SEQ], k, width, slice(c * P, (c + 1) * P), xh, xl, n_k,
                                None if c else stage)
            return last

        def tokens(k, bank, kk, t_hi, t_lo, start, stop):
            wh, wl = slot(k, D_MODEL)
            cols = slice(512 * (bank % 2), 512 * (bank % 2) + 512)
            for i, (x, w) in enumerate(((t_hi, wh), (t_hi, wl), (t_lo, wh))):
                last = pe.matmul(ps[:, bank, :], x, w[:, kk, cols], start=start and i == 0, stop=stop and i == 2,
                                 skip_group_check=True)
            return last

        def ffn(l, w):
            base = FFN_BASE[w]

            def gate_of(j, k, f):
                pe.wait_ge(w_lo, done_no(l, k, f))
                pe.wait_ge(silu_done, step_no(l, w, j) - 1)
                two_chunks(4, k).then_inc(w_used, 1)

            def up_of(j, k, f):
                pe.wait_ge(w_lo, done_no(l, k, f))
                if j is not None:
                    pe.wait_ge(prod_done, step_no(l, w, j))
                two_chunks(5, k).then_inc(w_used, 1)

            def down_of(j, k, f, last_one=False):
                pe.wait_ge(w_lo, done_no(l, k, f))
                pe.wait_ge(y_cleared, l * 2 + (w + 1))
                pe.wait_ge(hid_lo, step_no(l, w, j) + 1)
                src_hi, src_lo = (hhi_last, hlo_last) if last_one else (hhi, hlo)
                for bank in range(4):
                    for kk in range(2):
                        rows = slice(kk * SEQ + (bank // 2) * P, kk * SEQ + (bank // 2 + 1) * P)
                        last = tokens(k, bank, kk, src_hi[:, rows], src_lo[:, rows], False, True)
                    if last_one and bank < 3:
                        last.then_inc(y_bank, 1)
                last.then_inc(w_used, 1)

            pe.wait_ge(w_lo, done_no(l, base))
            two_chunks(4, base, stage=l * 3 + 2 * w).then_inc(w_used, 1)
            up_of(None, base + 1, 0)
            with pe.Fori(0, NF - 1) as f:
                gate_of(f + 1, base + 2, f)
                up_of(f + 1, base + 3, f)
                down_of(f, base + 4, f)
            down_of(NF - 1, base + 3 * NF - 1, 0, True)

        def layer_norm(l, w):
            for t in range(TT):
                for k in range(KC):
                    if k % 4 == 0:
                        pe.wait_ge(ln_rows1 if t else ln_rows0, l * 6 + (2 * w + k // 4 + 1))
                    last = pe.transpose(ps[:, 4 + k // 2, (k % 2) * SEQ + t * P:(k % 2) * SEQ + (t + 1) * P],
                                        z[:, t, k * P:(k + 1) * P], ident)
                    if t == 1 and k % 2:
                        last.then_inc(ln_turned, 1)

        def mixer(l):
            m0 = MIX_BASE

            def project(m, job):
                pe.wait_ge(w_lo, done_no(l, m0 + m))
                two_chunks(BANK[job], m0 + m).then_inc(w_used, 1)

            def half_tokens(m, jobs, cols):
                pe.wait_ge(w_lo, done_no(l, m0 + m))
                wh, wl = slot(m0 + m, 256)
                for t, job in enumerate(jobs):
                    tok = slice(t * P, (t + 1) * P)
                    for kk in range(KC):
                        last = tile3(ps[:, BANK[job], cols:cols + 256], xhi[:, kk, tok], xlo[:, kk, tok],
                                     wh[:, kk, :], wl[:, kk, :], kk == 0, kk == KC - 1)
                last.then_inc(w_used, 1)

            def latent(off):
                return (lambda kk: lhi[:, off + kk, :]), (lambda kk: llo[:, off + kk, :])

            def mla_scores(h):
                r = slice(64 * (h % 2), 64 * (h % 2) + 64)
                out = ps[:, BANK[f"S{h}"], :]
                for q, (lo_c, hi_c, n) in enumerate(((0, P, P), (P, 3 * P, SEQ))):
                    tok = slice(q * P, (q + 1) * P)
                    pe.matmul(out[:, lo_c:hi_c], q_nope[:, h, tok], k_nope[:, h, 0:n], start=True, stop=False)
                    last = pe.matmul(out[:, lo_c:hi_c], q_rope[r, h // 2, tok], k_rope[r, 0:n], start=False, stop=True)
                last.then_inc(s_done, 1)

            def mla_turn(h):
                pe.wait_ge(s_probs, l * 4 + (h + 1))
                for src in range(3):
                    last = pe.transpose(ps[:, BANK[f"T{h}"], src * P:(src + 1) * P],
                                        sc[:, h % 2, src * P:(src + 1) * P], ident)
                last.then_inc(p_turned, 1)

            def values(out, v, h, probs):
                cols = slice(h * DH, (h + 1) * DH)
                pe.matmul(out[:, 0:SEQ], v[:, 0, cols], probs[:, 0:SEQ], start=True, stop=False)
                return pe.matmul(out[:, P:SEQ], v[:, 1, cols], probs[:, SEQ:384], start=False, stop=True)

            def mla_values(p):
                for i in range(2):
                    pe.wait_ge(p_copied, l * 4 + (2 * p + i + 1))
                    last = values(ps[:, BANK[f"pv{p}"], i * SEQ:(i + 1) * SEQ], v_mla, 2 * p + i, pt[:, i, :])
                last.then_inc(mla_done, 1)

            def ret_values(p):
                for i in range(2):
                    pe.wait_ge(rt_probs, l * 4 + (2 * p + i + 1))
                    last = values(ps[:, BANK[f"rpv{p}"], i * SEQ:(i + 1) * SEQ], rv, 2 * p + i, pt[:, i, :])
                last.then_inc(rt_summed, 1)

            def key_scores(job, q, k, h):
                out = ps[:, BANK[job], :]
                pe.matmul(out[:, 0:SEQ], k[:, h, 0:P], q[:, h, :], start=True, stop=True)
                return pe.matmul(out[:, SEQ:384], k[:, h, P:SEQ], q[:, h, P:SEQ], start=True, stop=True)

            def ml_scores(h):
                key_scores(f"mS{h}", ml_qk[:, 0:4, :], ml_qk[:, 4:8, :], h).then_inc(ml_scored, 1)

            def ret_scores(h):
                key_scores(f"rS{h}", rq, rk, h).then_inc(rt_scored, 1)

            def ml_values(h):
                out, weights = ps[:, BANK[f"mpv{h}"], :], sc[:, h % 2, :]
                pe.wait_ge(ml_probs, l * 4 + (h + 1))
                values(out[:, 0:SEQ], ml_v, h, weights)
                pe.matmul(out[:, SEQ:], ones, weights[:, 0:SEQ], start=True, stop=False)
                pe.matmul(out[:, SEQ + P:], ones, weights[:, SEQ:384], start=False, stop=True).then_inc(ml_summed, 1)

            def spread(h):
                pe.matmul(ps[:, BANK[f"bc{h}"], :], C("sel", P, h * P)[0:HEADS, :], row_m[:, :],
                          start=True, stop=True).then_inc(bc_done, 1)

            def means(n):
                pe.matmul(ps[:, BANK[f"{'mr'[n // 2]}_mean{n % 2}"], :], ones, ht[:, n % 2, :],
                          start=True, stop=True).then_inc(h_means, 1)

            def variances(n):
                pe.wait_ge(h_squared, l * 4 + (n + 1))
                pe.matmul(ps[:, BANK[f"{'mr'[n // 2]}_var{n % 2}"], :], ones, ht_sq[:, :],
                          start=True, stop=True).then_inc(h_vars, 1)

            pe.wait_ge(w_lo, done_no(l, m0))
            two_chunks(BANK["c0"], m0, stage=l * 3 + 1).then_inc(w_used, 1)
            project(1, "c1")
            pe.wait_ge(w_lo, done_no(l, m0 + 2))
            features(ps[:, BANK["c2"], 0:SEQ], m0 + 2, 192, slice(0, P), x_h, x_l, KC)
            last = features(ps[0:ROPE, BANK["c2"], SEQ:], m0 + 2, 192, slice(P, 192), x_h, x_l, KC)
            last.then_inc(w_used, 1)
            project(3, "qk0")
            pe.wait_ge(lat_squared, l * 3 + 3)
            for c in range(QC):
                pe.matmul(ps[:, BANK["rms"], 0:SEQ], ones, lat_sq[:, c, :], start=c == 0, stop=c == QC - 1)
            for c in range(QC, QC + VC):
                last = pe.matmul(ps[:, BANK["rms"], SEQ:], ones, lat_sq[:, c, :], start=c == QC,
                                 stop=c == QC + VC - 1)
            last.then_inc(lat_summed, 1)
            pe.wait_ge(lat_copied, l * 3 + 1)
            project(4, "qk1")
            pe.wait_ge(lat_copied, l * 3 + 2)
            project(5, "qk2")
            pe.wait_ge(rot_copied, l * 6 + 1)
            project(6, "qk3")

            pe.wait_ge(lat_lo, l + 1)
            q_h, q_l = latent(0)
            for i in range(2):
                k = m0 + 7 + i
                pe.wait_ge(w_lo, done_no(l, k))
                if i == 0:
                    pe.wait_ge(conv_copied, l * 4 + 2)
                else:
                    pe.wait_ge(conv_copied, l * 4 + 3)
                two_chunks(BANK[f"qn{i}"], k, 384, QC, q_h, q_l)
                features(ps[:, BANK["qr"], i * SEQ:(i + 1) * SEQ], k, 384, slice(2 * P, 3 * P), q_h, q_l, QC)\
                    .then_inc(w_used, 1)
            k = m0 + 9
            k_h, k_l = latent(QC)
            pe.wait_ge(w_lo, done_no(l, k))
            for i in range(2):
                if i == 0:
                    pe.wait_ge(conv_copied, l * 4 + 4)
                else:
                    pe.wait_ge(q_copied, l * 2 + 1)
                for c in range(2):
                    last = features(ps[:, BANK[f"kn{i}"], c * SEQ:(c + 1) * SEQ], k, 1024,
                                    slice(256 * (2 * i + c), 256 * (2 * i + c) + P), k_h, k_l, VC)
            last.then_inc(k_done, 1)
            wv = [t[:, k % RING, 0:VC * 1024].rearrange("p (k h n) -> p k h n", h=HEADS, n=256) for t in (whi, wlo)]
            for t in range(TT):
                if t == 0:
                    pe.wait_ge(rot_copied, l * 6 + 2)
                else:
                    pe.wait_ge(q_copied, l * 2 + 2)
                tok = slice(t * P, (t + 1) * P)
                for kk in range(VC):
                    last = tile3(ps[:, BANK[f"v{t}"], :], lhi[:, QC + kk, tok], llo[:, QC + kk, tok],
                                 wv[0][:, kk, :, P:256], wv[1][:, kk, :, P:256], kk == 0, kk == VC - 1)
            last.then_inc(w_used, 1)
            pe.wait_ge(k_copied, l * 2 + 2)
            half_tokens(10, ("mv0", "mv1"), 0)
            half_tokens(11, ("mv0", "mv1"), 256)
            pe.wait_ge(w_lo, done_no(l, m0 + 12))
            pe.wait_ge(v_copied, l * 6 + 1)
            for i in range(2):
                last = features(ps[0:HEADS, BANK["gates"], i * SEQ:(i + 1) * SEQ], m0 + 12, 2 * HEADS,
                                slice(i * HEADS, (i + 1) * HEADS), x_h, x_l, KC)
            last.then_inc(w_used, 1)

            pe.wait_ge(rotated, l * 6 + 2)
            mla_scores(0)
            mla_scores(1)
            pe.wait_ge(v_copied, l * 6 + 2)
            project(13, "rq0")
            mla_turn(0)
            pe.wait_ge(lat_std, l + 1)
            mla_turn(1)
            pe.wait_ge(v_copied, l * 6 + 3)
            project(14, "rq1")
            pe.wait_ge(s_masked, l * 4 + 1)
            mla_values(0)
            pe.wait_ge(s_masked, l * 4 + 2)
            mla_scores(2)
            pe.wait_ge(p_copied, l * 4 + 1)
            mla_scores(3)
            pe.wait_ge(p_copied, l * 4 + 2)
            pe.wait_ge(a_row_ready, l + 1)
            for t in range(TT):
                last = pe.matmul(ps[:, BANK["aT"], t * HEADS:(t + 1) * HEADS], row_i[:, t * P:(t + 1) * P],
                                 ident[0:HEADS, 0:HEADS], start=True, stop=True)
            last.then_inc(a_turned, 1)
            pe.wait_ge(v_copied, l * 6 + 4)
            project(15, "rk0")
            pe.wait_ge(y_lo, l * 6 + 1)
            mla_turn(2)
            pe.wait_ge(s_masked, l * 4 + 3)
            mla_turn(3)
            pe.wait_ge(floor_ready, l + 1)
            pe.wait_ge(s_masked, l * 4 + 4)
            spread(0)
            pe.wait_ge(a_copied, l + 1)
            spread(1)
            pe.wait_ge(f_pre, l + 1)
            project(16, "rk1")
            pe.wait_ge(p_copied, l * 4 + 3)
            mla_values(1)
            pe.wait_ge(qk_silu, l * 2 + 2)
            pe.wait_ge(p_copied, l * 4 + 4)
            ml_scores(0)
            pe.wait_ge(bc_copied, l * 4 + 1)
            ml_scores(1)
            pe.wait_ge(rot_copied, l * 6 + 4)
            half_tokens(17, ("rv0", "rv1"), 0)
            pe.wait_ge(bc_copied, l * 4 + 2)
            ml_values(0)
            pe.wait_ge(y_lo, l * 6 + 2)
            ml_values(1)
            pe.wait_ge(ml_probs, l * 4 + 2)
            spread(2)
            spread(3)
            half_tokens(18, ("rv0", "rv1"), 256)
            pe.wait_ge(h_ready, l * 4 + 2)
            means(0)
            ml_scores(2)
            pe.wait_ge(bc_copied, l * 4 + 3)
            ml_scores(3)
            pe.wait_ge(rot_copied, l * 6 + 5)
            project(19, "mo0")
            pe.wait_ge(bc_copied, l * 4 + 4)
            variances(0)
            pe.wait_ge(h_centred, l * 4 + 1)
            ml_values(2)
            pe.wait_ge(ml_probs, l * 4 + 3)
            ml_values(3)
            pe.wait_ge(rotated, l * 6 + 6)
            pe.wait_ge(ml_probs, l * 4 + 4)
            ret_scores(0)
            pe.wait_ge(h_std, l * 4 + 1)
            ret_scores(1)
            pe.wait_ge(rot_copied, l * 6 + 6)
            project(20, "mo1")
            pe.wait_ge(h_ready, l * 4 + 4)
            means(1)
            pe.wait_ge(v_copied, l * 6 + 6)
            ret_values(0)
            ret_scores(2)
            ret_scores(3)
            project(21, "rg0")
            pe.wait_ge(h_centred, l * 4 + 2)
            variances(1)
            pe.wait_ge(rt_copied, l * 2 + 1)
            means(2)
            pe.wait_ge(rt_probs, l * 4 + 3)
            ret_values(1)
            project(22, "rg1")

            for b in range(3):
                turn = l * 3 + b
                for h in range(2):
                    for i in range(2):
                        k = m0 + 23 + 6 * b + 3 * h + i
                        pe.wait_ge(w_lo, done_no(l, k))
                        pe.wait_ge(gates_ready, turn * 4 + (2 + i if h else 1))
                        if b == h == 0:
                            pe.wait_ge(rg_ready, l * 2 + 2)
                        two_chunks(4 + i, k).then_inc(w_used, 1)
                        if b == h == i == 0:
                            pe.wait_ge(rt_probs, l * 4 + 4)
                            variances(2)
                            pe.wait_ge(h_std, l * 4 + 2)
                            pe.wait_ge(rt_copied, l * 2 + 2)
                            means(3)
                        elif b == h == 0:
                            pe.wait_ge(h_centred, l * 4 + 3)
                            variances(3)
                    k = m0 + 25 + 6 * b + 3 * h
                    pe.wait_ge(w_lo, done_no(l, k))
                    if h and b:
                        pe.wait_ge(gate_used, l * 8 + (4 * b - 2))
                    elif h:
                        pe.wait_ge(branch_added, turn * 4 + 3)
                    else:
                        pe.wait_ge(branch_added, turn * 4 + 1)
                        pe.wait_ge(y_lo, l * 6 + (2 * b + 2))
                    for c in range(4):
                        last = features(ps[:, 6 + c // 2, (c % 2) * SEQ:(c % 2 + 1) * SEQ], k, 512,
                                        slice(c * P, (c + 1) * P), lambda kk: yhi[:, b, kk, :],
                                        lambda kk: ylo[:, b, kk, :], HEADS)
                    last.then_inc(w_used, 1)
            for i in range(MIX_OUT):
                k = m0 + 41 + i
                pe.wait_ge(w_lo, done_no(l, k))
                pe.wait_ge(m_lo, l * 4 + (i + 1))
                for bank in range(4):
                    tok = slice((bank // 2) * P, (bank // 2 + 1) * P)
                    for kk in range(2):
                        chunk = 2 * i + kk
                        last = tokens(k, bank, kk, mhi[:, chunk, tok], mlo[:, chunk, tok], chunk == 0, chunk == KC - 1)
                    if i == MIX_OUT - 1 and bank < 3:
                        last.then_inc(y_bank, 1)
                last.then_inc(w_used, 1)

        pe.wait_ge(square_loaded, 16)
        for t in range(TT):
            pe.wait_ge(x_loaded, 16 * TT)
            for k in range(KC):
                last = pe.transpose(ps[:, 4 + k // 2, (k % 2) * SEQ + t * P:(k % 2) * SEQ + (t + 1) * P],
                                    xtok[:, t, k * P:(k + 1) * P], ident)
        last.then_inc(x_turned, 1)

        with pe.Fori(0, DEPTH) as l:
            ffn(l, 0)
            layer_norm(l, 0)
            mixer(l)
            layer_norm(l, 1)
            ffn(l, 1)
            layer_norm(l, 2)

    ctx.close()


def lay_out(inputs):
    a = {n: np.ascontiguousarray(inputs[n]) for n in (
        "x", "positions", "w_in", "mla_w_ukv", "w_out",
        "ffn1_w_gate", "ffn1_w_up", "ffn1_w_down", "ffn2_w_gate", "ffn2_w_up", "ffn2_w_down")}
    a["w_br"] = np.stack([np.asarray(inputs[f"w_br_{n}"]) for n in ("mla", "mlstm", "ret")], axis=1)
    uq = np.asarray(inputs["mla_w_uq"]).reshape(DEPTH, Q_LORA, 2, 2, DH + ROPE)
    a["mla_w_uq"] = np.concatenate([uq[..., :DH].reshape(DEPTH, Q_LORA, 2, 2 * DH),
                                    uq[..., DH:].reshape(DEPTH, Q_LORA, 2, 2 * ROPE)], axis=3)\
        .reshape(DEPTH, Q_LORA, -1)
    ln = [[np.asarray(inputs[f"ln{i}_{c}"]) for c in "gb"] for i in (1, 2, 3)]
    a["ln_rows"] = np.stack([np.stack(pair, axis=1) for pair in ln], axis=1)

    def columns(v):
        return np.asarray(v).reshape(DEPTH, -1, P).transpose(0, 2, 1)

    def rows_as_column(v):
        out = np.zeros((DEPTH, P, 1), np.float32)
        out[:, :HEADS, 0] = v
        return out

    gate_b = np.asarray(inputs["mlstm_gate_b"])
    parts = dict(
        ln_g=columns(np.concatenate([g for g, _ in ln], axis=1)),
        ln_b=columns(np.concatenate([b for _, b in ln], axis=1)),
        q_g=columns(inputs["mla_q_norm_g"]), kv_g=columns(inputs["mla_kv_norm_g"]),
        conv_w=columns(np.asarray(inputs["mlstm_conv_w"]).reshape(DEPTH, -1)),
        conv_b=columns(inputs["mlstm_conv_b"]),
        ml_g=columns(inputs["mlstm_norm_g"]), rt_g=columns(inputs["ret_norm_g"]),
        gate_b=columns(np.asarray(inputs["gate_b"]).reshape(DEPTH, -1)),
        i_b=rows_as_column(gate_b[:, :HEADS]), f_b=rows_as_column(gate_b[:, HEADS:]))
    assert all(parts[n].shape[2] == s for n, s in PARAM_SIZES.items())
    a["params"] = np.concatenate([parts[n] for n in PARAM_SIZES], axis=2)
    a["consts"] = constants()
    return {n: np.ascontiguousarray(v) for n, v in a.items()}


def kernel(**inputs):
    import concourse.bacc as bacc
    from concourse.bass_utils import run_bass_kernel_spmd

    arrays = lay_out(inputs)
    nc = bacc.Bacc("TRN2", target_bir_lowering=False, num_devices=1)
    a = {n: nc.dram_tensor(n, v.shape, mybir.dt.from_np(v.dtype), kind="ExternalInput").ap()
         for n, v in arrays.items()}
    a["out"] = nc.dram_tensor("out", (1, SEQ, D_MODEL), F32, kind="ExternalOutput").ap()
    build(nc, a)
    r = run_bass_kernel_spmd(nc, [arrays], core_ids=[0])
    return r.results[0]["out"]
```
